# Optimizing a Trainium2 kernel written in Bass

```python
import jax, jax.numpy as jnp
from jax import lax
import numpy as np

D_MODEL = 2048
BATCH = 1
SEQ = 256
DEPTH = 1

MEM_LEN = 256
EPS = 1e-6
D_FF = 5504
MLA_HEADS = 8
MLA_NOPE = 128
MLA_ROPE = 64
MLA_QK = MLA_NOPE + MLA_ROPE
MLA_V = 128
MLA_Q_RANK = 512
MLA_KV_RANK = 256
ROPE_BASE = 10000.0
Q_BLOCK = 128
HG_HEADS = 8
HG_DK = 128
HG_DV = 128
HG_CHUNK = 64
MLA_WIDTH = MLA_HEADS * MLA_V
HG_WIDTH = HG_HEADS * HG_DV
MIX_WIDTH = MLA_WIDTH + HG_WIDTH
HG_KW = HG_HEADS * HG_DK
IN_SIZES = (MLA_Q_RANK, MLA_KV_RANK, MLA_ROPE, HG_KW, HG_KW, HG_WIDTH, HG_WIDTH)
IN_COLS = int(sum(IN_SIZES))
IN_SPLITS = [int(v) for v in np.cumsum(IN_SIZES)[:-1]]
MEM_HEADS = 4
MEM_HD = 128
MEM_WIDTH = MEM_HEADS * MEM_HD

kernel_name = "hymba_mla_hgrn2_macaron_layer"

def rmsnorm(x, g):
    xf = x.astype(jnp.float32)
    y = xf * lax.rsqrt(jnp.mean(xf * xf, axis=-1, keepdims=True) + EPS)
    return (y * g.astype(jnp.float32)).astype(x.dtype)

def swiglu(h, w_gate, w_up, w_down):
    return (jax.nn.silu(h @ w_gate) * (h @ w_up)) @ w_down

def rope(x, positions):
    half = MLA_ROPE // 2
    inv_freq = ROPE_BASE ** (-jnp.arange(half, dtype=jnp.float32) / half)
    ang = positions.astype(jnp.float32)[..., None] * inv_freq
    cos = jnp.cos(ang)[:, :, None, :]
    sin = jnp.sin(ang)[:, :, None, :]
    xf = x.astype(jnp.float32)
    x1, x2 = xf[..., :half], xf[..., half:]
    out = jnp.concatenate([x1 * cos - x2 * sin, x2 * cos + x1 * sin], axis=-1)
    return out.astype(x.dtype)

def mla_group(cq, ckv, kpe, positions, q_a_norm, w_q_up, kv_a_norm, w_kv_up, q_norm, k_norm, out_norm):
    B, S, _ = cq.shape
    q = (rmsnorm(cq, q_a_norm) @ w_q_up).reshape(B, S, MLA_HEADS, MLA_QK)
    kv = (rmsnorm(ckv, kv_a_norm) @ w_kv_up).reshape(B, S, MLA_HEADS, MLA_NOPE + MLA_V)
    k_nope, v = kv[..., :MLA_NOPE], kv[..., MLA_NOPE:]
    k_pe = jnp.broadcast_to(kpe[:, :, None, :], (B, S, MLA_HEADS, MLA_ROPE))
    k = jnp.concatenate([k_nope, k_pe], axis=-1)
    q = rmsnorm(q, q_norm)
    k = rmsnorm(k, k_norm)
    q = jnp.concatenate([q[..., :MLA_NOPE], rope(q[..., MLA_NOPE:], positions)], axis=-1)
    k = jnp.concatenate([k[..., :MLA_NOPE], rope(k[..., MLA_NOPE:], positions)], axis=-1)
    scale = MLA_QK ** -0.5
    nb = S // Q_BLOCK
    qb = q.reshape(B, nb, Q_BLOCK, MLA_HEADS, MLA_QK).transpose(1, 0, 2, 3, 4)
    kpos = jnp.arange(S)

    def attend(args):
        qblk, i = args
        qpos = i * Q_BLOCK + jnp.arange(Q_BLOCK)
        s = jnp.einsum('bqhd,bkhd->bhqk', qblk, k, preferred_element_type=jnp.float32) * scale
        s = jnp.where(kpos[None, :] <= qpos[:, None], s, -jnp.inf)
        p = jax.nn.softmax(s, axis=-1).astype(v.dtype)
        return jnp.einsum('bhqk,bkhd->bqhd', p, v)

    o = lax.map(attend, (qb, jnp.arange(nb)))
    o = o.transpose(1, 0, 2, 3, 4).reshape(B, S, MLA_WIDTH)
    return rmsnorm(o, out_norm)

def hgrn2_group(qx, fx, ix, gx, lb, out_norm):
    B, S, _ = qx.shape
    dtype = qx.dtype
    lbf = lb.astype(jnp.float32)
    f = lbf + (1.0 - lbf) * jax.nn.sigmoid(fx.astype(jnp.float32))
    logf = jnp.log(f)
    kx = 1.0 - f
    nc = S // HG_CHUNK

    def heads(t, d):
        return t.astype(jnp.float32).reshape(B, nc, HG_CHUNK, HG_HEADS, d).transpose(1, 0, 3, 2, 4)

    q, k, lf, v = heads(qx, HG_DK), heads(kx, HG_DK), heads(logf, HG_DK), heads(ix, HG_DV)
    causal = jnp.tril(jnp.ones((HG_CHUNK, HG_CHUNK), dtype=bool))

    def step(state, inp):
        qc, kc, vc, lfc = inp
        b = jnp.cumsum(lfc, axis=2)
        o_inter = jnp.einsum('bhtk,bhkv->bhtv', qc * jnp.exp(b), state)
        diff = b[:, :, :, None, :] - b[:, :, None, :, :]
        decay = jnp.exp(jnp.where(causal[None, None, :, :, None], diff, -jnp.inf))
        a = jnp.einsum('bhtk,bhsk,bhtsk->bhts', qc, kc, decay)
        o = o_inter + jnp.einsum('bhts,bhsv->bhtv', a, vc)
        b_last = b[:, :, -1:, :]
        k_dec = kc * jnp.exp(b_last - b)
        new_state = jnp.exp(b_last[:, :, 0, :])[..., None] * state + jnp.einsum('bhsk,bhsv->bhkv', k_dec, vc)
        return new_state, o

    s0 = jnp.zeros((B, HG_HEADS, HG_DK, HG_DV), jnp.float32)
    _, o = lax.scan(step, s0, (q, k, v, lf))
    o = o.transpose(1, 0, 3, 2, 4).reshape(B, S, HG_HEADS, HG_DV)
    o = rmsnorm(o, out_norm) * jax.nn.silu(gx.astype(jnp.float32).reshape(B, S, HG_HEADS, HG_DV))
    return o.reshape(B, S, HG_WIDTH).astype(dtype)

def memory_xattn(h, m, w_q, w_kv, q_norm, k_norm, w_o):
    B, S, _ = h.shape
    M = m.shape[1]
    q = rmsnorm((h @ w_q).reshape(B, S, MEM_HEADS, MEM_HD), q_norm)
    kv = (m @ w_kv).reshape(B, M, MEM_HEADS, 2 * MEM_HD)
    k = rmsnorm(kv[..., :MEM_HD], k_norm)
    v = kv[..., MEM_HD:]
    s = jnp.einsum('bshd,bmhd->bhsm', q, k, preferred_element_type=jnp.float32) * (MEM_HD ** -0.5)
    p = jax.nn.softmax(s, axis=-1).astype(v.dtype)
    o = jnp.einsum('bhsm,bmhd->bshd', p, v).reshape(B, S, MEM_WIDTH)
    return o @ w_o

def setup_inputs(seed: int = 0) -> dict:
    key = jax.random.key(seed)
    ks = iter(jax.random.split(key, 40))
    f32 = jnp.float32

    def w(shape, fan_in):
        return jax.random.normal(next(ks), shape, f32) * (fan_in ** -0.5)

    def gain(shape):
        return 1.0 + 0.02 * jax.random.normal(next(ks), shape, f32)

    L = DEPTH
    x = jax.random.normal(next(ks), (BATCH, SEQ, D_MODEL), f32)
    mem = jax.random.normal(next(ks), (BATCH, MEM_LEN, D_MODEL), f32)
    offset = jax.random.randint(next(ks), (BATCH, 1), 0, 4096, dtype=jnp.int32)
    positions = offset + jnp.arange(SEQ, dtype=jnp.int32)[None, :]
    return {
        "x": x, "mem": mem, "positions": positions,
        "ffn1_norm": gain((L, D_MODEL)),
        "ffn1_w_gate": w((L, D_MODEL, D_FF), D_MODEL),
        "ffn1_w_up": w((L, D_MODEL, D_FF), D_MODEL),
        "ffn1_w_down": w((L, D_FF, D_MODEL), D_FF),
        "mix_norm": gain((L, D_MODEL)),
        "w_in": w((L, D_MODEL, IN_COLS), D_MODEL),
        "mla_q_a_norm": gain((L, MLA_Q_RANK)),
        "mla_w_q_up": w((L, MLA_Q_RANK, MLA_HEADS * MLA_QK), MLA_Q_RANK),
        "mla_kv_a_norm": gain((L, MLA_KV_RANK)),
        "mla_w_kv_up": w((L, MLA_KV_RANK, MLA_HEADS * (MLA_NOPE + MLA_V)), MLA_KV_RANK),
        "mla_q_norm": gain((L, MLA_QK)),
        "mla_k_norm": gain((L, MLA_QK)),
        "mla_out_norm": gain((L, MLA_WIDTH)),
        "hg_lb_logits": 0.1 * jax.random.normal(next(ks), (L + 1, HG_KW), f32),
        "hg_out_norm": gain((L, HG_DV)),
        "w_out": w((L, MIX_WIDTH, D_MODEL), MIX_WIDTH),
        "xattn_norm": gain((L, D_MODEL)),
        "mem_norm": gain((L, D_MODEL)),
        "xattn_w_q": w((L, D_MODEL, MEM_WIDTH), D_MODEL),
        "xattn_w_kv": w((L, D_MODEL, 2 * MEM_WIDTH), D_MODEL),
        "xattn_q_norm": gain((L, MEM_HD)),
        "xattn_k_norm": gain((L, MEM_HD)),
        "xattn_w_o": w((L, MEM_WIDTH, D_MODEL), MEM_WIDTH),
        "ffn2_norm": gain((L, D_MODEL)),
        "ffn2_w_gate": w((L, D_MODEL, D_FF), D_MODEL),
        "ffn2_w_up": w((L, D_MODEL, D_FF), D_MODEL),
        "ffn2_w_down": w((L, D_FF, D_MODEL), D_FF),
    }

def reference(x, mem, positions,
              ffn1_norm, ffn1_w_gate, ffn1_w_up, ffn1_w_down,
              mix_norm, w_in,
              mla_q_a_norm, mla_w_q_up, mla_kv_a_norm, mla_w_kv_up, mla_q_norm, mla_k_norm, mla_out_norm,
              hg_lb_logits, hg_out_norm,
              w_out,
              xattn_norm, mem_norm, xattn_w_q, xattn_w_kv, xattn_q_norm, xattn_k_norm, xattn_w_o,
              ffn2_norm, ffn2_w_gate, ffn2_w_up, ffn2_w_down):
    lb_all = jnp.cumsum(jax.nn.softmax(hg_lb_logits.astype(jnp.float32), axis=0), axis=0)
    for l in range(DEPTH):
        h = rmsnorm(x, ffn1_norm[l])
        x = x + 0.5 * swiglu(h, ffn1_w_gate[l], ffn1_w_up[l], ffn1_w_down[l])
        h = rmsnorm(x, mix_norm[l])
        proj = h @ w_in[l]
        cq, ckv, kpe, hq, hf, hi, hg = jnp.split(proj, IN_SPLITS, axis=-1)
        a = mla_group(cq, ckv, kpe, positions, mla_q_a_norm[l], mla_w_q_up[l], mla_kv_a_norm[l],
                      mla_w_kv_up[l], mla_q_norm[l], mla_k_norm[l], mla_out_norm[l])
        r = hgrn2_group(hq, hf, hi, hg, lb_all[l], hg_out_norm[l])
        x = x + jnp.concatenate([a, r], axis=-1) @ w_out[l]
        h = rmsnorm(x, xattn_norm[l])
        m = rmsnorm(mem, mem_norm[l])
        x = x + memory_xattn(h, m, xattn_w_q[l], xattn_w_kv[l], xattn_q_norm[l], xattn_k_norm[l], xattn_w_o[l])
        h = rmsnorm(x, ffn2_norm[l])
        x = x + 0.5 * swiglu(h, ffn2_w_gate[l], ffn2_w_up[l], ffn2_w_down[l])
    return x


_drawn_inputs = setup_inputs


def setup_inputs(seed=0):
    import zlib

    import numpy as np

    out = dict(_drawn_inputs(seed))
    spreads = {}
    factors = {'ffn1_norm': 5.224,
     'mla_q_a_norm': 5.668,
     'mla_kv_a_norm': 3.891,
     'mla_q_norm': 5.332,
     'mla_k_norm': 5.814,
     'mla_out_norm': 5.181,
     'hg_out_norm': 8.0,
     'xattn_norm': 8.0,
     'mem_norm': 8.0,
     'xattn_q_norm': 8.0,
     'xattn_k_norm': 8.0,
     'ffn2_norm': 8.0}
    for name, (base, spread) in spreads.items():
        noise = np.random.default_rng([zlib.crc32(name.encode()), seed]).standard_normal(out[name].shape)
        drawn = base * np.exp(spread * noise) if base else spread * noise
        out[name] = __import__('jax').numpy.asarray(drawn.astype(out[name].dtype))
    for name, factor in factors.items():
        out[name] = (out[name] * factor).astype(out[name].dtype)
    return out
```

```python
from contextlib import ExitStack

import numpy as np

import concourse.bass as bass
from concourse import mybir

F32 = mybir.dt.float32
F32R = mybir.dt.float32r
I32 = mybir.dt.int32
U8 = mybir.dt.uint8
ALU = mybir.AluOpType
ACT = mybir.ActivationFunctionType
AX = mybir.AxisListType.X

P = 128
NW = 512
RAW = 4
SPLIT = 2
EPS = 1e-6
RH = 32
LEVELS = 8
TWO_PI = 2 * np.pi
PI_1 = 6.28125
PI_2 = float(np.float32(round((TWO_PI - PI_1) * 2 ** 20) / 2 ** 20))
PI_3 = TWO_PI - PI_1 - PI_2
ROUND = 1.5 * 2 ** 23


class Done:

    def __init__(self, eng, sem):
        self.eng, self.sem, self.n = eng, sem, 0

    def __call__(self, ins):
        ins.then_inc(self.sem, 1)
        self.n += 1

    def wait(self):
        if self.n:
            self.eng.wait_ge(self.sem, self.n)


def down_tiles(tiles):
    return [tiles // 8 + (s < tiles % 8) for s in range(8)]


def over(ap, n):
    return ap.unsqueeze(2).broadcast_to([ap.shape[0], ap.shape[1], n])


def under(ap, n):
    return ap.unsqueeze(1).broadcast_to([ap.shape[0], n, ap.shape[1]])


def layer(nc, a, out):
    SEQ, D = a["x"].shape[1:]
    MEM = a["mem"].shape[1]
    FF = a["ffn1_w_gate"].shape[2]
    TT, MT = SEQ // P, MEM // P
    KD, DB = D // P, D // NW
    FT, FA = FF // P, 24
    HALVES = ((0, FA), (FA, FT - FA))
    ROPE = 2 * RH
    QR = a["mla_q_a_norm"].shape[1] // P
    KR = a["mla_kv_a_norm"].shape[1] // P
    QK = a["mla_q_norm"].shape[1]
    AH = a["mla_w_q_up"].shape[2] // QK
    HG = a["hg_lb_logits"].shape[1] // P
    HH = HG // 2
    XH = a["xattn_w_o"].shape[1] // P
    SCALE, X_SCALE = float(QK) ** -0.5, float(P) ** -0.5

    ctx = ExitStack()
    with ctx:
        def sb(name, shape, dt=F32):
            return ctx.enter_context(nc.sbuf_tensor(name, shape, dt))

        def sem(name):
            return ctx.enter_context(nc.semaphore(name))

        x = sb("x_res", [P, TT, D])
        raw = sb("w_raw", [P, RAW, 4 * NW])
        w_hi = sb("w_hi", [P, SPLIT, 4 * NW], F32R)
        w_lo = sb("w_lo", [P, SPLIT, 4 * NW], F32R)
        stage = sb("stage", [P, 2 * TT, NW])
        gate, nat = stage[:, 0:TT, :], stage[:, TT:2 * TT, :]
        memkT = sb("memkT", [P, XH, MEM])
        memv = sb("memv", [P, MT, XH * P])
        ident = sb("ident", [P, P])
        gains = sb("gains", [P, P])
        level_mask = sb("level_mask", [P, LEVELS, P], U8)
        causal = sb("causal", [P, SEQ])
        one = sb("one", [P, 1])
        cs = sb("cos_sin", [P, 2, TT, RH])
        pe_gain = sb("pe_gain", [P, 2, ROPE])
        bound = sb("bound", [P, 2, HG])
        sums = sb("sums", [P, 82])
        means = sb("means", [P, 82])
        rsq = sb("rsq", [P, 82])
        half = sb("minus_half", [P, 16])
        smax = sb("score_max", [P, 2, 4])
        ssum = sb("score_sum", [P, 2, 4])
        srec = sb("score_rec", [P, 2, 4])

        KB = 1024
        slab_bytes = 106 * KB + 512
        base = -(-nc.sbuf_base // 64) * 64
        sb("slab_fence", [P, (slab_bytes + base - nc.sbuf_base) // 4])

        def at(name, kb, shape, dt=F32):
            n = 4
            for v in shape[1:]:
                n *= v
            assert kb * KB + n <= slab_bytes, name
            return nc.alloc_sbuf_tensor_at(name, shape, dt, offset=base + int(kb * KB))

        hT_hi = at("hT_hi", 0, [P, KD, SEQ], F32R)
        hT_lo = at("hT_lo", 16, [P, KD, SEQ], F32R)
        q_nat = at("q_nat", 0, [P, TT, AH * QK])
        kv_nat = at("kv_nat", 12, [P, TT, AH * 2 * P])
        q_pe = at("q_pe", 28, [P, TT, AH, ROPE])
        probT = at("probT", 0, [P, 2, 6 * P])
        A0 = 32
        actT_hi = at("actT_hi", A0, [P, FA, SEQ], F32R)
        actT_lo = at("actT_lo", A0 + 24, [P, FA, SEQ], F32R)
        mT_hi, mT_lo = actT_hi, actT_lo
        mem_nat = at("mem_nat", A0 + 48, [P, MT, D])
        memkv = at("memkv", A0 + 48, [P, 2 * MT, NW])
        memk = at("memk", A0 + 56, [P, 4 * MT, P])
        mem_rows = at("mem_gain_rows", A0 + 64, [P, P])
        rows = at("gain_rows", A0 + 64.5, [P, P])
        pos_i = at("pos_i", A0 + 65, [P, TT], I32)
        pos_f = at("pos_f", A0 + 65.0625, [P, TT])
        freq = at("freq", A0 + 65.125, [P, RH])
        ang = at("ang", A0 + 65.5, [P, 2, TT * RH])
        turns = at("turns", A0 + 66, [P, 2, TT * RH])
        rest = at("rest", A0 + 66.5, [P, 2, TT * RH])
        lbt = at("lbt", A0 + 67, [P, 6, HG])
        mask_i = at("mask_i", A0 + 68, [P, LEVELS, P], I32)
        bT = at("bT", A0, [P, 4, SEQ])
        kxT = at("kxT", A0 + 4, [P, 4, SEQ])
        qxT = at("qxT", A0 + 8, [P, 4, SEQ])
        lfT = at("lfT", A0 + 12, [P, 4, SEQ])
        wave = at("wave", A0 + 16, [P, 2, 4 * SEQ])
        AT = at("AT", A0 + 24, [P, HG, 3, P])
        V = at("V", A0 + 36, [P, TT, HG * P])
        G = at("G", A0 + 44, [P, TT, HG * P])
        cqT_hi = at("cqT_hi", A0 + 52, [P, QR, SEQ], F32R)
        cqT_lo = at("cqT_lo", A0 + 56, [P, QR, SEQ], F32R)
        ckvT_hi = at("ckvT_hi", A0 + 60, [P, KR, SEQ], F32R)
        ckvT_lo = at("ckvT_lo", A0 + 62, [P, KR, SEQ], F32R)
        ckv_nat = at("ckv_nat", A0 + 64, [P, TT, KR * P + ROPE])
        o_hg = at("o_hg", A0 + 66.5, [P, TT, HG * P])
        qTn = at("qTn", A0, [P, AH, SEQ])
        kTn = at("kTn", A0 + 8, [P, AH, SEQ])
        qTp = [at("qTp_even", A0 + 16, [P, AH // 2, SEQ]), at("qTp_odd", 6, [P, AH // 2, SEQ])]
        kTp = at("kTp", A0 + 20, [P, AH // 2, SEQ])
        k_pe = at("k_pe", A0 + 56, [P, TT, AH, ROPE])
        k_rot = at("k_rot", A0 + 60, [P, TT, ROPE])
        o_mla = at("o_mla", A0 + 56, [P, TT, AH * P])
        catT_hi = at("catT_hi", A0 + 24, [P, 16, SEQ], F32R)
        catT_lo = at("catT_lo", A0 + 40, [P, 16, SEQ], F32R)
        xqT = at("xqT", A0, [P, XH, SEQ])
        x_probT = at("x_probT", A0 + 4, [P, 2, TT, 4 * P])
        xo = at("xo", A0 + 12, [P, TT, XH * P])
        xoT_hi = at("xoT_hi", A0 + 16, [P, XH, SEQ], F32R)
        xoT_lo = at("xoT_lo", A0 + 20, [P, XH, SEQ], F32R)

        acc = ctx.enter_context(nc.psum_tensor("acc", [P, 2, TT, NW], F32))
        tr = ctx.enter_context(nc.psum_tensor("tr", [P, 2, NW], F32))
        small = ctx.enter_context(nc.psum_tensor("small", [P, 2, NW], F32))


        loaded = [sem(f"raw_loaded{s}") for s in range(RAW)]
        hi_done = sem("hi_done")
        lo_done = sem("lo_done")
        slot_used = sem("slot_used")
        acc_taken = [sem("acc_taken0"), sem("acc_taken1")]
        tr_ready = [sem("tr_ready0"), sem("tr_ready1")]
        tr_taken = [sem("tr_taken0"), sem("tr_taken1")]
        t_hi = sem("turned_hi")
        small_ready = [sem("small_ready0"), sem("small_ready1")]
        small_taken = [sem("small_taken0"), sem("small_taken1")]
        dve_done, act_done, pool_done = sem("dve_done"), sem("act_done"), sem("pool_done")
        mem_rows_in, rows_in, const_in, x_in = sem("mem_gain_rows_in"), sem("gain_rows_in"), sem("const_in"), sem("x_in")
        mem_in = [sem(f"mem_in{j}") for j in range(D // NW)]
        out_done = sem("out_done")
        named = {}

        def ev(name):
            if name not in named:
                named[name] = sem(name)
            return named[name]

        GAIN_ROWS = [("mem_norm", KD), ("ffn1_norm", KD), ("mix_norm", KD), ("xattn_norm", KD), ("ffn2_norm", KD),
                     ("mla_out_norm", AH), ("hg_lb_logits", 2 * HG), ("mla_q_a_norm", QR), ("mla_kv_a_norm", KR),
                     ("xattn_q_norm", 1), ("xattn_k_norm", 1), ("hg_out_norm", 1), ("mla_q_norm", 1), ("mla_k_norm", 1)]
        col, N_ROWS = {}, 0
        for name, n in GAIN_ROWS:
            col[name] = N_ROWS
            N_ROWS += n

        NORMS = {"mem": (MT, D), "x1": (TT, D), "memk": (2 * MT * 2, P), "x2": (TT, D), "cq": (TT, QR * P), "ckv": (TT, KR * P),
                 "q": (TT * AH, QK), "k": (TT * AH, QK), "hg": (TT * HG, P), "o_mla": (TT, AH * P), "x3": (TT, D),
                 "xq": (TT * XH, P), "x4": (TT, D)}
        at_col, c = {}, 0
        for name, (n, _) in NORMS.items():
            at_col[name] = c
            c += n
        KPE = c

        def cols(t, name, i=0, n=None):
            c = at_col[name] + i
            return t[:, c:c + (NORMS[name][0] if n is None else n)]

        slots, blocks, groups, splits, fills = {}, {}, {}, {}, {}
        count = {}

        def number(table, name, n=1):
            table[name] = count.get(id(table), 0)
            count[id(table)] = table[name] + n

        def number_ffn(f):
            for h in range(2):
                pairs = -(-HALVES[h][1] // 4)
                number(slots, (f, "up", h), 8 * pairs)
                number(blocks, (f, "up", h), 2 * pairs)
                number(groups, (f, "up", h), pairs)
                number(splits, (f, "up", h), pairs)
                number(slots, (f, "down", h), 8 * DB)
                number(blocks, (f, "down", h), DB)
                if h == 1 and f == 1:
                    number(groups, (f, "down", h), DB)
                    number(splits, (f, "down", h), DB)

        MIX = ["hf0", "hq0", "cq", "ckv", "hi0", "hi1", "hf1", "hq1", "hg0", "hg1"]
        STEPS = LEVELS + 1
        STEP0 = {0: 11, 1: 36}

        number(groups, "mem", DB)
        number(splits, "mem", DB)
        number(slots, "memkv", 8)
        number(blocks, "memkv", 2)
        number(groups, "x", DB)
        number(splits, "x", DB)
        number(groups, "memk")
        number_ffn(1)
        number(slots, "mix", 4 * len(MIX))
        number(blocks, "mix", len(MIX))
        for n in ("hf0", "hq0", "cq", "ckv", "hf1", "hq1"):
            number(groups, n)
        for n in ("cq", "ckv"):
            number(splits, n)
        number(slots, "q_up", 3)
        number(blocks, "q_up", 3)
        number(slots, "kv_up", 2)
        number(blocks, "kv_up", 4)
        number(fills, "steps", 2 * STEPS)
        number(fills, "av", 2)
        for n in ("qn", "kn"):
            number(groups, n, 2)
        for n in ("qp", "kp"):
            number(groups, n)
        number(groups, "cat_hg", 2)
        number(splits, "cat_hg", 2)
        number(fills, "mla", 2 * (AH // 2))
        number(groups, "prob", AH // 2)
        number(slots, "w_out", 4 * DB)
        number(blocks, "w_out", DB)
        number(groups, "cat_mla", 2)
        number(splits, "cat_mla", 2)
        number(groups, "x_out", DB)
        number(splits, "x_out", DB)
        number(slots, "xq", 4)
        number(blocks, "xq", 1)
        number(groups, "xq")
        number(fills, "xattn", 2 * (XH // 2))
        number(groups, "x_prob", XH // 2)
        number(groups, "xo")
        number(splits, "xo")
        number(slots, "w_o", DB)
        number(blocks, "w_o", DB)
        number(groups, "x_o", DB)
        number(splits, "x_o", DB)
        number_ffn(2)
        M = slots["mix"]
        FILL_ORDER = ([0, 1, 3, 5], [2, 4, 6, 7])

        ENTRY = {"x2": ((1, "down", 1), "mix_norm"), "x3": ("x_out", "xattn_norm"), "x4": ("x_o", "ffn2_norm")}
        LAST_BLOCK = {"x2": blocks[1, "down", 1] + DB - 1, "x3": blocks["w_out"] + DB - 1, "x4": blocks["w_o"] + DB - 1}
        FACTOR = {"x2": 0.5, "x3": 1.0, "x4": 1.0}
        MIX_WIDTH = {n: NW for n in MIX}
        MIX_WIDTH["ckv"] = KR * P + ROPE
        starts = {"cq": 0, "ckv": QR * P}
        q0 = QR * P + KR * P + ROPE
        for i, n in enumerate(("hq", "hf", "hi", "hg")):
            for h in range(2):
                starts[f"{n}{h}"] = q0 + (2 * i + h) * NW

        block = ctx.enter_context(nc.Block())

        @block.sync
        def _(sp):
            def load(c, rep, src, tiles, width):
                if c >= RAW:
                    sp.wait_ge(lo_done, c + rep - RAW + 1)
                dst = raw[:, c % RAW, 0:tiles * width].rearrange("p (k n) -> p k n", k=tiles)
                sp.dma_start(dst, src).then_inc(loaded[c % RAW], 16)

            def rows_of(w, k0, tiles, cols):
                return w[k0 * P:(k0 + tiles) * P, cols].rearrange("(k p) n -> p k n", p=P)

            def load_ffn(f):
                wg, wu, wd = (a[f"ffn{f}_w_{n}"][0] for n in ("gate", "up", "down"))
                for h, (f0, tiles) in enumerate(HALVES):
                    c0, full = slots[f, "up", h], tiles // 4

                    def pair(c, rep, cols, width):
                        for b, w in enumerate((wg, wu)):
                            for s in range(4):
                                load(c + 4 * b + s, rep, rows_of(w, 4 * s, 4, cols), 4, width)
                    with sp.Fori(0, full) as i:
                        pair(c0, 8 * i, bass.ds(i * NW + f0 * P, NW), NW)
                    if tiles % 4:
                        width = (tiles % 4) * P
                        pair(c0 + 8 * full, 0, bass.ds((f0 + 4 * full) * P, width), width)
                    cd = slots[f, "down", h]
                    with sp.Fori(0, DB) as j:
                        k = f0
                        for s, n in enumerate(down_tiles(tiles)):
                            load(cd + s, 8 * j, rows_of(wd, k, n, bass.ds(j * NW, NW)), n, NW)
                            k += n

            def load_gains(i):
                name, n = GAIN_ROWS[i]
                src = a[name] if name == "hg_lb_logits" else a[name][0:1, 0:n * P]
                dst, r0 = (rows, col[name] - KD) if i else (mem_rows, 0)
                sp.dma_start(dst[r0:r0 + n, :], src.rearrange("l (r p) -> (l r) p", p=P)).then_inc(rows_in if i else mem_rows_in, 16)

            def load_mem(j):
                sp.dma_start(mem_nat[:, :, j * NW:(j + 1) * NW],
                             a["mem"][0].rearrange("(t p) n -> p t n", p=P)[:, :, j * NW:(j + 1) * NW]).then_inc(mem_in[j], 16)

            def load_memkv(c):
                b, s = divmod(c, 4)
                load(slots["memkv"] + c, 0, rows_of(a["xattn_w_kv"][0], 4 * s, 4, slice(b * NW, (b + 1) * NW)), 4, NW)

            sp.dma_start(ident[:], a["ident"]).then_inc(mem_rows_in, 16)
            load_mem(0)
            load_gains(0)
            load_memkv(0)
            for j in range(1, DB):
                load_mem(j)
                load_memkv(j)
            for i in range(1, len(GAIN_ROWS)):
                load_gains(i)
            for t in range(TT):
                sp.dma_start(x[:, t, :], a["x"][0, t * P:(t + 1) * P, :]).then_inc(x_in, 16)
            for c in range(DB, 8):
                load_memkv(c)
            sp.dma_start(mask_i[:], a["level_mask"]).then_inc(const_in, 16)
            sp.dma_start(causal[:], a["causal"]).then_inc(const_in, 16)
            sp.dma_start(freq[:], a["freq"]).then_inc(const_in, 16)
            with nc.allow_non_contiguous_dma(reason="one position for each partition"):
                for t in range(TT):
                    sp.dma_start(pos_i[:, t:t + 1], a["positions"][0, t * P:(t + 1) * P].rearrange("(p o) -> p o", o=1)).then_inc(const_in, 16)
            for n, name in enumerate(("mla_q_norm", "mla_k_norm")):
                sp.dma_start(pe_gain[:, n, :], a[name][0:1, P:QK].broadcast_to([P, ROPE])).then_inc(const_in, 16)
            load_ffn(1)
            for b, n in enumerate(MIX):
                for s in range(4):
                    load(M + 4 * b + s, 0, rows_of(a["w_in"][0], 4 * s, 4, slice(starts[n], starts[n] + MIX_WIDTH[n])), 4, MIX_WIDTH[n])
            for b in range(3):
                load(slots["q_up"] + b, 0, rows_of(a["mla_w_q_up"][0], 0, QR, slice(b * NW, (b + 1) * NW)), QR, NW)
            for b in range(2):
                load(slots["kv_up"] + b, 0, rows_of(a["mla_w_kv_up"][0], 0, KR, slice(2 * b * NW, 2 * (b + 1) * NW)), KR, 2 * NW)
            for j in range(DB):
                for s, k in enumerate((8, 12, 0, 4)):
                    load(slots["w_out"] + 4 * j + s, 0, rows_of(a["w_out"][0], k, 4, slice(j * NW, (j + 1) * NW)), 4, NW)
            for s in range(4):
                load(slots["xq"] + s, 0, rows_of(a["xattn_w_q"][0], 4 * s, 4, slice(0, NW)), 4, NW)
            for j in range(DB):
                load(slots["w_o"] + j, 0, rows_of(a["xattn_w_o"][0], 0, 4, slice(j * NW, (j + 1) * NW)), 4, NW)
            load_ffn(2)
            for j in range(DB):
                B = blocks[2, "down", 1] + j
                sp.wait_ge(acc_taken[B % 2], B // 2 + 1)
                sp.dma_start(out[0].rearrange("(t p) n -> p t n", p=P)[:, :, j * NW:(j + 1) * NW],
                             x[:, :, j * NW:(j + 1) * NW]).then_inc(out_done, 16)
            sp.wait_ge(out_done, 16 * DB)

        @block.gpsimd
        def _(pool):
            done = Done(pool, pool_done)

            def norm(name):
                n, width = NORMS[name]
                pool.wait_ge(ev("sums_" + name), 1)
                done(nc.gpsimd.tensor_scalar(cols(means, name), cols(sums, name), 1.0 / width, EPS, ALU.mult, ALU.add))
                done.wait()
                nc.gpsimd.tensor_tensor(cols(rsq, name), cols(means, name), half[:, 0:n], ALU.pow).then_inc(ev("rsq_" + name), 1)

            def complement(h):
                pool.wait_ge(ev("forget"), h + 1)
                if h:
                    pool.wait_ge(small_ready[1], STEPS)
                nc.gpsimd.tensor_scalar(kxT[:], bT[:], -1.0, 1.0, ALU.mult, ALU.add).then_inc(ev("complement"), 1)

            def differences(k):
                h, l = divmod(k, STEPS)
                if l == 0:
                    return
                if l == 1:
                    pool.wait_ge(ev("running"), h + 1)
                if k >= 2:
                    pool.wait_ge(small_ready[1], k - 1)
                m = 2 ** (l - 1)
                w = wave[:, k % 2, :].rearrange("p (n u m) -> p n u m", u=2, m=m)
                b = bT[:].rearrange("p h t -> p (h t)").rearrange("p (n u m) -> p n u m", u=2, m=m)
                mid = over(b[:, :, 0, m - 1], m)
                nc.gpsimd.tensor_tensor(w[:, :, 1, :], b[:, :, 1, :], mid, ALU.subtract)
                nc.gpsimd.tensor_tensor(w[:, :, 0, :], mid, b[:, :, 0, :], ALU.subtract).then_inc(ev("differences"), 1)

            done(nc.gpsimd.memset(half[:], -0.5))
            done.wait()
            norm("mem")
            norm("x1")
            kv = memkv[:].rearrange("p r (h c) -> p r h c", h=2)
            pool.wait_ge(ev("memkv"), 2)
            for b in range(2):
                for t in range(MT):
                    ins = nc.gpsimd.tensor_copy(memv[:, t, 2 * b * P:2 * (b + 1) * P].rearrange("p (h c) -> p h c", h=2),
                                                kv[:, b * MT + t, :, P:2 * P])
            ins.then_inc(ev("memv"), 1)
            norm("memk")
            norm("x2")
            complement(0)
            for k in range(STEPS):
                differences(k)
            norm("cq")
            norm("ckv")
            complement(1)
            for k in range(STEPS, 2 * STEPS):
                differences(k)
            for name in ("q", "k", "hg", "o_mla", "x3", "xq", "x4"):
                norm(name)

        @block.scalar
        def _(act):
            done = Done(act, act_done)
            flat_stage = stage[:].rearrange("p a b -> p (a b)")

            def hi(c, rep, tiles, width):
                act.wait_ge(loaded[c % RAW], 16 * (c // RAW + 1) + rep * (16 // RAW))
                if c >= SPLIT:
                    act.wait_ge(slot_used, c + rep - SPLIT + 1)
                n = tiles * width
                nc.scalar.activation(w_hi[:, c % SPLIT, 0:n], raw[:, c % RAW, 0:n], ACT.Copy).then_inc(hi_done, 1)

            def turned_hi(dst, tile0, g, rep, gain=None, tiles=4, step=1):
                for b in range(2):
                    m0, n = b * -(-tiles // 2), (-(-tiles // 2), tiles // 2)[b]
                    act.wait_ge(tr_ready[b], g + rep + 1)
                    if gain is None or step == 0:
                        ins = nc.scalar.activation(dst[:, bass.ds(tile0 + m0, n), :], tr[:, b, 0:n * SEQ].rearrange("p (k t) -> p k t", k=n),
                                                   ACT.Copy, scale=1.0 if gain is None else gains[:, gain:gain + 1])
                    else:
                        for m in range(n):
                            k = tile0 + m0 + m
                            ins = nc.scalar.activation(dst[:, k, :], tr[:, b, m * SEQ:(m + 1) * SEQ], ACT.Copy,
                                                       scale=gains[:, gain + k:gain + k + 1])
                    ins.then_inc(t_hi, 1)

            def turned(dst, tile0, g, gain=None):
                for b in range(2):
                    act.wait_ge(tr_ready[b], g + 1)
                    ins = nc.scalar.activation(dst[:, tile0 + 2 * b:tile0 + 2 * b + 2, :], tr[:, b, :].rearrange("p (k t) -> p k t", k=2),
                                               ACT.Copy, scale=1.0 if gain is None else gains[:, gain:gain + 1])
                    ins.then_inc(tr_taken[b], 1)

            def square_sums(name, src):
                for t in range(src.shape[1]):
                    done.wait()
                    ins = nc.scalar.activation(flat_stage[:, 0:src.shape[2]], src[:, t, :], ACT.Square, accum_out=cols(sums, name, t, 1))
                    if t == 0:
                        done(ins)
                ins.then_inc(ev("sums_" + name), 1)
                act.wait_ge(ev("sums_" + name), 1)

            def take(B, c_end, dst, func, scale, width=NW):
                act.wait_ge(slot_used, c_end)
                for t in range(TT):
                    ins = nc.scalar.activation(dst(t), acc[:, B % 2, t, 0:width], func, scale=scale[:, t:t + 1])
                ins.then_inc(acc_taken[B % 2], 1)

            def entry(name, s):
                key, gain = ENTRY[name]
                if s == 2:
                    turned_hi(hT_hi, 4 * (DB - 1), groups[key] + DB - 1, 0, gain=col[gain])
                if s == 3:
                    B = LAST_BLOCK[name]
                    act.wait_ge(acc_taken[B % 2], B // 2 + 1)
                    square_sums(name, x)

            def ffn(f, name):
                for h, (f0, tiles) in enumerate(HALVES):
                    c0, b0, g0 = slots[f, "up", h], blocks[f, "up", h], groups[f, "up", h]
                    full = tiles // 4

                    def pair(i, k, width=NW):
                        c, rep, prev = c0 + 8 * k, 8 * i, k > 0
                        for s in range(6):
                            if not (f == 2 and h == 0 and not prev and s == 0):
                                hi(c + s, rep, 4, width)
                            if prev and s == 3:
                                turned_hi(actT_hi, 4 * (i + k - 1), g0 + k - 1, i)
                            if not prev and h == 0 and f == 2:
                                entry(name, s)
                            if not prev and h == 0 and f == 1 and s == 1:
                                take_memkv(1)
                            if not prev and h == 0 and f == 1 and s == 5:
                                bound_and_angles()
                        if prev:
                            act.wait_ge(acc_taken[(b0 + 1) % 2], (b0 + 1) // 2 + k + i)
                        elif h == 0:
                            act.wait_ge(ev("rsq_" + name), 1)
                        act.wait_ge(slot_used, c + rep + 4)
                        for t in range(TT):
                            ins = nc.scalar.activation(gate[:, t, 0:width], acc[:, b0 % 2, t, 0:width], ACT.Silu, scale=cols(rsq, name, t, 1))
                        ins.then_inc(acc_taken[b0 % 2], 1)
                        if not prev and h == 0 and f == 1:
                            turned(memkT, 0, groups["memk"], gain=col["xattn_k_norm"])
                        hi(c + 6, rep, 4, width)
                        hi(c + 7, rep, 4, width)

                    pair(0, 0)
                    with act.Fori(0, full - 1) as i:
                        pair(i, 1)
                    last = full - 1
                    if tiles % 4:
                        last = full
                        pair(0, full, (tiles % 4) * P)
                    cd = slots[f, "down", h]
                    ns = down_tiles(tiles)
                    for j in range(DB):
                        for s in range(8):
                            hi(cd + 8 * j + s, 0, ns[s], NW)
                            if j == 0 and s == 3:
                                turned_hi(actT_hi, 4 * last, g0 + last, 0, tiles=tiles - 4 * last)
                            if j > 0 and s == 4 and h == 1 and f == 1:
                                turned_hi(hT_hi, 4 * (j - 1), groups[f, "down", h] + j - 1, 0, gain=col["mix_norm"])

            def bound_and_angles():
                act.wait_ge(ev("lb_shifted"), 1)
                nc.scalar.activation(lbt[:, 3:5, :], lbt[:, 1:3, :], ACT.Exp).then_inc(ev("lb_exp"), 1)
                act.wait_ge(ev("angles"), 1)
                nc.scalar.activation(cs[:].rearrange("p k t f -> p k (t f)"), rest[:], ACT.Sin).then_inc(ev("cos_sin"), 1)

            def take_memkv(b):
                if b == 0:
                    act.wait_ge(ev("rsq_mem"), 1)
                take(blocks["memkv"] + b, slots["memkv"] + 4 * b + 4, lambda t: memkv[:, b * MT + t, :], ACT.Copy, cols(rsq, "mem"))
                act.wait_ge(acc_taken[(blocks["memkv"] + b) % 2], (blocks["memkv"] + b) // 2 + 1)
                act.sem_inc(ev("memkv"), 1)

            def mem_turned(j):
                turned_hi(mT_hi, 4 * j, groups["mem"] + j, 0, gain=col["mem_norm"])

            def x_turned(j):
                turned_hi(hT_hi, 4 * j, groups["x"] + j, 0, gain=col["ffn1_norm"])

            act.wait_ge(ev("gains"), 1)
            for j in range(2):
                mem_turned(j)
                hi(j, 0, 4, NW)
            for j in range(2, DB):
                hi(j, 0, 4, NW)
                mem_turned(j)
            hi(4, 0, 4, NW)
            square_sums("mem", mem_nat)
            act.wait_ge(ev("gains"), 2)
            for j in range(3):
                hi(5 + j, 0, 4, NW)
                x_turned(j)
                if j == 0:
                    take_memkv(0)
                if j == 1:
                    square_sums("x1", x)
            x_turned(3)
            ffn(1, "x1")

            def mixer(m):
                if m < 4:
                    entry("x2", m)
                if m >= 5 and (m - 5) % 4 == 0 and (m - 5) // 4 < len(MIX):
                    b = (m - 5) // 4
                    n = MIX[b]
                    kind, h = n[:2], n[-1]
                    if b == 0:
                        act.wait_ge(ev("rsq_x2"), 1)
                    dst, func = {
                        "hf": (lambda t: gate[:, t, :], ACT.Sigmoid), "hq": (lambda t: nat[:, t, :], ACT.Copy),
                        "cq": (lambda t: gate[:, t, :], ACT.Copy), "ck": (lambda t: ckv_nat[:, t, :], ACT.Copy),
                        "hi": (lambda t: V[:, t, int(h) * NW:(int(h) + 1) * NW], ACT.Copy),
                        "hg": (lambda t: G[:, t, int(h) * NW:(int(h) + 1) * NW], ACT.Silu)}[kind]
                    take(blocks["mix"] + b, M + 4 * b + 4, dst, func, cols(rsq, "x2"), MIX_WIDTH[n])
                    if n in ("cq", "ckv"):
                        act.wait_ge(acc_taken[(blocks["mix"] + b) % 2], (blocks["mix"] + b) // 2 + 1)
                        src = gate if n == "cq" else ckv_nat[:, :, 0:KR * P]
                        if n == "ckv":
                            act.wait_ge(ev("sums_cq"), 1)
                        for t in range(TT):
                            ins = nc.scalar.activation(nat[:, t, 0:src.shape[2]], src[:, t, :], ACT.Square, accum_out=cols(sums, n, t, 1))
                        ins.then_inc(ev("sums_" + n), 1)
                for h, m0 in ((0, 6), (1, 30)):
                    if m == m0:
                        act.wait_ge(ev("forget"), h + 1)
                        nc.scalar.activation(lfT[:], bT[:], ACT.Ln).then_inc(ev("log_forget"), 1)
                    if m == m0 + 4:
                        turned(qxT, 0, groups[f"hq{h}"])
                if m == 14:
                    turned_hi(cqT_hi, 0, groups["cq"], 0, gain=col["mla_q_a_norm"])
                if m == 18:
                    turned_hi(ckvT_hi, 0, groups["ckv"], 0, gain=col["mla_kv_a_norm"], tiles=KR)
                for h in range(2):
                    l = m - STEP0[h]
                    if 1 <= l < STEPS:
                        k = h * STEPS + l
                        act.wait_ge(ev("differences"), h * (STEPS - 1) + l)
                        nc.scalar.activation(wave[:, k % 2, :], wave[:, k % 2, :], ACT.Exp).then_inc(ev("decays"), 1)
                for b in range(3):
                    if m == 42 + b:
                        if b == 0:
                            act.wait_ge(ev("rsq_cq"), 1)
                        take(blocks["q_up"] + b, slots["q_up"] + b + 1, lambda t: q_nat[:, t, b * NW:(b + 1) * NW], ACT.Copy, cols(rsq, "cq"))
                for b in range(2):
                    if m == 45 + b:
                        if b == 0:
                            act.wait_ge(ev("rsq_ckv"), 1)
                        take(blocks["kv_up"] + 2 * b, slots["kv_up"] + b + 1, lambda t: kv_nat[:, t, 2 * b * NW:(2 * b + 1) * NW],
                             ACT.Copy, cols(rsq, "ckv"))

            for m in range(40):
                hi(M + m, 0, 4, MIX_WIDTH[MIX[m // 4]])
                mixer(m)
            for m in range(40, 47):
                hi(M + m, 0, 4, NW)
                mixer(m)

            B = blocks["q_up"] + 2
            act.wait_ge(acc_taken[B % 2], B // 2 + 1)
            for t in range(TT):
                dst = (flat_stage, o_hg[:].rearrange("p a b -> p (a b)"))[t][:, 0:AH * QK]
                nc.scalar.activation(dst, q_nat[:, t, :], ACT.Square).then_inc(ev("q_squares"), 1)
            for B in (blocks["kv_up"] + 2, blocks["kv_up"] + 3):
                act.wait_ge(acc_taken[B % 2], B // 2 + 1)
            act.wait_ge(ev("sums_q"), 1)
            for t in range(TT):
                nc.scalar.activation(flat_stage[:, t * AH * P:(t + 1) * AH * P].rearrange("p (h c) -> p h c", h=AH),
                                     kv_nat[:, t, :].rearrange("p (h c) -> p h c", h=AH)[:, :, 0:P], ACT.Square).then_inc(ev("k_squares"), 1)
            for h in range(2):
                for t in range(TT):
                    act.wait_ge(small_ready[t], fills["av"] + h + 1)
                    if h == 0 and t == 0:
                        act.wait_ge(ev("sums_k"), 1)
                    nc.scalar.activation(stage[:, 2 * h + t, :], small[:, t, :], ACT.Square).then_inc(ev("hg_squares"), 1)
            for n, dst, g in (("qn", qTn, "mla_q_norm"), ("kn", kTn, "mla_k_norm")):
                for i in range(2):
                    turned(dst, 4 * i, groups[n] + i, gain=col[g])
            for b in range(2):
                act.wait_ge(tr_ready[b], groups["qp"] + 1)
                for n in range(2):
                    r = slice(n * ROPE, (n + 1) * ROPE)
                    ins = nc.scalar.activation(qTp[n][r, 2 * b:2 * b + 2, :], tr[r, b, :].rearrange("p (k t) -> p k t", k=2), ACT.Copy)
                ins.then_inc(tr_taken[b], 1)
            turned(kTp, 0, groups["kp"])
            for i in range(2):
                turned_hi(catT_hi, 8 + 4 * i, groups["cat_hg"] + i, 0, gain=col["hg_out_norm"], step=0)

            def exps(p):
                act.wait_ge(ev("shifted"), p + 1)
                nc.scalar.activation(flat_stage[:, (p % 2) * 1024:(p % 2) * 1024 + 6 * P], flat_stage[:, (p % 2) * 1024:(p % 2) * 1024 + 6 * P],
                                     ACT.Exp, scale=SCALE).then_inc(ev("exps"), 1)

            def prob_turned(p):
                g = groups["prob"] + p
                for b in range(2):
                    n = (4, 2)[b] * P
                    act.wait_ge(tr_ready[b], g + 1)
                    nc.scalar.activation(probT[:, p % 2, 4 * P * b:4 * P * b + n], tr[:, b, 0:n], ACT.Copy).then_inc(tr_taken[b], 1)

            NP_ = AH // 2
            exps(0)
            for p in range(NP_):
                if p + 1 < NP_:
                    exps(p + 1)
                prob_turned(p)
            act.wait_ge(ev("o_mla"), NP_)
            square_sums("o_mla", o_mla)
            for i in range(2):
                turned_hi(catT_hi, 4 * i, groups["cat_mla"] + i, 0, gain=col["mla_out_norm"])

            for j in range(DB):
                for s in range(4):
                    if j or s >= 2:
                        hi(slots["w_out"] + 4 * j + s, 0, 4, NW)
                    if j and s == 2:
                        turned_hi(hT_hi, 4 * (j - 1), groups["x_out"] + j - 1, 0, gain=col["xattn_norm"])

            for s in range(4):
                hi(slots["xq"] + s, 0, 4, NW)
                entry("x3", s)
            for s in range(2):
                hi(slots["w_o"] + s, 0, 4, NW)
            act.wait_ge(ev("rsq_x3"), 1)
            take(blocks["xq"], slots["xq"] + 4, lambda t: gate[:, t, :], ACT.Copy, cols(rsq, "x3"))
            act.wait_ge(acc_taken[blocks["xq"] % 2], blocks["xq"] // 2 + 1)
            nc.scalar.activation(nat, gate, ACT.Square).then_inc(ev("xq_squares"), 1)
            turned(xqT, 0, groups["xq"], gain=col["xattn_q_norm"])
            for p in range(XH // 2):
                act.wait_ge(ev("x_shifted"), p + 1)
                nc.scalar.activation(stage[:, 2 * p:2 * p + 2, :], stage[:, 2 * p:2 * p + 2, :], ACT.Exp, scale=X_SCALE).then_inc(ev("x_exps"), 1)
            for p in range(XH // 2):
                for t in range(TT):
                    act.wait_ge(tr_ready[t], groups["x_prob"] + p + 1)
                    nc.scalar.activation(x_probT[:, p, t, :], tr[:, t, :], ACT.Copy).then_inc(tr_taken[t], 1)
            turned_hi(xoT_hi, 0, groups["xo"], 0)
            for j in range(2, DB):
                hi(slots["w_o"] + j, 0, 4, NW)
            turned_hi(hT_hi, 0, groups["x_o"], 0, gain=col["ffn2_norm"])
            hi(slots[2, "up", 0], 0, 4, NW)
            for j in range(1, DB - 1):
                turned_hi(hT_hi, 4 * j, groups["x_o"] + j, 0, gain=col["ffn2_norm"])
            ffn(2, "x4")

        @block.vector
        def _(dve):
            done = Done(dve, dve_done)
            v = nc.vector
            flat_stage = stage[:].rearrange("p a b -> p (a b)")

            def lo(c, rep, tiles, width):
                dve.wait_ge(hi_done, c + rep + 1)
                n = tiles * width
                v.tensor_tensor(w_lo[:, c % SPLIT, 0:n], raw[:, c % RAW, 0:n],
                                w_hi[:, c % SPLIT, 0:n].bitcast(F32), ALU.subtract).then_inc(lo_done, 1)

            def turned_lo(dst_hi, dst, tile0, g, rep, h, hrep, gain=None, tiles=4, step=1):
                for b in range(2):
                    m0, n = b * -(-tiles // 2), (-(-tiles // 2), tiles // 2)[b]
                    dve.wait_ge(t_hi, 2 * h + b + 1 + 2 * hrep)
                    at_, src = bass.ds(tile0 + m0, n), tr[:, b, 0:n * SEQ].rearrange("p (k t) -> p k t", k=n)
                    if gain is None:
                        ins = v.tensor_tensor(dst[:, at_, :], src, dst_hi[:, at_, :].bitcast(F32), ALU.subtract)
                    elif step == 0:
                        ins = v.scalar_tensor_tensor(dst[:, at_, :], src, gains[:, gain:gain + 1], dst_hi[:, at_, :].bitcast(F32),
                                                     ALU.mult, ALU.subtract)
                    else:
                        for m in range(n):
                            k = tile0 + m0 + m
                            ins = v.scalar_tensor_tensor(dst[:, k, :], src[:, m, :], gains[:, gain + k:gain + k + 1],
                                                         dst_hi[:, k, :].bitcast(F32), ALU.mult, ALU.subtract)
                    ins.then_inc(tr_taken[b], 1)

            def add_block(B, c_end, j, factor):
                dve.wait_ge(slot_used, c_end)
                for t in range(TT):
                    ins = v.scalar_tensor_tensor(x[:, t, j * NW:(j + 1) * NW], acc[:, B % 2, t, :], factor,
                                                 x[:, t, j * NW:(j + 1) * NW], ALU.mult, ALU.add)
                ins.then_inc(acc_taken[B % 2], 1)

            def entry(name, s, c):
                key, gain = ENTRY[name]
                if s == 1:
                    add_block(LAST_BLOCK[name], c, DB - 1, FACTOR[name])
                if s == 2:
                    turned_lo(hT_hi, hT_lo, 4 * (DB - 1), groups[key] + DB - 1, 0, splits[key] + DB - 1, 0, gain=col[gain])

            def ffn(f, name):
                for h, (f0, tiles) in enumerate(HALVES):
                    c0, b0, g0, h0 = slots[f, "up", h], blocks[f, "up", h], groups[f, "up", h], splits[f, "up", h]
                    full = tiles // 4

                    def up(i, k, width):
                        B = b0 + 1
                        dve.wait_ge(slot_used, c0 + 8 * k + 8 + 8 * i)
                        dve.wait_ge(acc_taken[b0 % 2], b0 // 2 + k + 1 + i)
                        for t in range(TT):
                            ins = v.scalar_tensor_tensor(nat[:, t, 0:width], acc[:, B % 2, t, 0:width], cols(rsq, name, t, 1),
                                                         gate[:, t, 0:width], ALU.mult, ALU.mult)
                        ins.then_inc(acc_taken[B % 2], 1)

                    def pair(i, k, width=NW):
                        c, rep, prev = c0 + 8 * k, 8 * i, k > 0
                        for s in range(8):
                            if not (f == 2 and h == 0 and not prev and s == 0):
                                lo(c + s, rep, 4, width)
                            if prev and s == 1:
                                up(i, k - 1, NW)
                            if prev and s == 3:
                                turned_lo(actT_hi, actT_lo, 4 * (i + k - 1), g0 + k - 1, i, h0 + k - 1, i)
                            if not prev and h == 1 and s == 1:
                                add_block(b0 - 1, c0, DB - 1, 0.5)
                            if not prev and h == 0 and f == 2:
                                entry(name, s, c0)
                            if not prev and h == 0 and f == 1:
                                memory_keys(s)
                                if s == 4:
                                    angles()
                                if s == 7:
                                    lower_bound()

                    pair(0, 0)
                    with dve.Fori(0, full - 1) as i:
                        pair(i, 1)
                    width, last = NW, full - 1
                    if tiles % 4:
                        width, last = (tiles % 4) * P, full
                        pair(0, full, width)
                    cd, bd = slots[f, "down", h], blocks[f, "down", h]
                    ns = down_tiles(tiles)
                    for j in range(DB):
                        for s in range(8):
                            lo(cd + 8 * j + s, 0, ns[s], NW)
                            if j == 0 and s == 1:
                                up(0, last, width)
                            if j == 0 and s == 3:
                                turned_lo(actT_hi, actT_lo, 4 * last, g0 + last, 0, h0 + last, 0, tiles=tiles - 4 * last)
                            if j > 0 and s == 1:
                                add_block(bd + j - 1, cd + 8 * j, j - 1, 0.5)
                            if j > 0 and s == 4 and h == 1 and f == 1:
                                turned_lo(hT_hi, hT_lo, 4 * (j - 1), groups[f, "down", h] + j - 1, 0, splits[f, "down", h] + j - 1, 0,
                                          gain=col["mix_norm"])

            def memory_keys(s):
                k = memkv[:].rearrange("p r (h c) -> p (r h) c", h=2)[:, :, 0:P]
                if s == 2:
                    dve.wait_ge(ev("memkv"), 2)
                    done(v.tensor_tensor(memk[:], k, k, ALU.mult))
                    done.wait()
                    v.tensor_reduce(cols(sums, "memk"), memk[:], AX, ALU.add).then_inc(ev("sums_memk"), 1)
                if s == 3:
                    dve.wait_ge(ev("rsq_memk"), 1)
                    dve.wait_ge(ev("sums_memk"), 1)
                    v.tensor_tensor(memk[:], k, over(cols(rsq, "memk"), P), ALU.mult).then_inc(ev("memk"), 1)

            def angles():
                L = gains[:, col["hg_lb_logits"]:col["hg_lb_logits"] + 2 * HG].rearrange("p (l h) -> p l h", l=2)
                done(v.tensor_tensor(lbt[:, 0, :], L[:, 0, :], L[:, 1, :], ALU.max))
                done.wait()
                v.tensor_tensor(lbt[:, 1:3, :], L, under(lbt[:, 0, :], 2), ALU.subtract).then_inc(ev("lb_shifted"), 1)
                dve.wait_ge(const_in, 16 * (3 + TT + 2))
                done(v.tensor_copy(level_mask[:], mask_i[:]))
                done(v.tensor_copy(pos_f[:], pos_i[:]))
                done.wait()
                for k in range(2):
                    for t in range(TT):
                        done(v.tensor_scalar(ang[:, k, t * RH:(t + 1) * RH], freq[:], pos_f[:, t:t + 1], None, ALU.mult))
                done.wait()
                for k in range(2):
                    done(v.tensor_scalar(turns[:, k, :], ang[:, k, :], 1.0 / TWO_PI, 0.25 * k, ALU.mult, ALU.add))
                for shift in (ROUND, -ROUND):
                    done.wait()
                    done(v.tensor_scalar(turns[:], turns[:], shift, None, ALU.add))
                done.wait()
                for n, part in enumerate((PI_1, PI_2, PI_3)):
                    done(v.scalar_tensor_tensor(rest[:], turns[:], -part, ang[:] if n == 0 else rest[:], ALU.mult, ALU.add))
                    done.wait()
                done(v.tensor_scalar(rest[:, 1, :], rest[:, 1, :], TWO_PI / 4, None, ALU.add))
                done.wait()
                v.tensor_scalar(rest[:], rest[:], 3.1415925, -3.1415925, ALU.min, ALU.max).then_inc(ev("angles"), 1)

            def lower_bound():
                dve.wait_ge(ev("lb_exp"), 1)
                done(v.tensor_tensor(lbt[:, 5, :], lbt[:, 3, :], lbt[:, 4, :], ALU.add))
                done.wait()
                done(v.reciprocal(lbt[:, 0, :], lbt[:, 5, :]))
                done.wait()
                done(v.tensor_tensor(bound[:, 0, :], lbt[:, 3, :], lbt[:, 0, :], ALU.mult))
                done.wait()
                done(v.tensor_scalar(bound[:, 1, :], bound[:, 0, :], -1.0, 1.0, ALU.mult, ALU.add))

            dve.wait_ge(ev("gains_turned"), 1)
            v.tensor_copy(gains[:, 0:KD], small[:, 0, 0:KD]).then_inc(ev("gains"), 1)
            dve.wait_ge(ev("gains"), 1)

            def mem_lo(j):
                turned_lo(mT_hi, mT_lo, 4 * j, groups["mem"] + j, 0, splits["mem"] + j, 0, gain=col["mem_norm"])

            def x_lo(j):
                turned_lo(hT_hi, hT_lo, 4 * j, groups["x"] + j, 0, splits["x"] + j, 0, gain=col["ffn1_norm"])

            for j in range(2):
                mem_lo(j)
                lo(j, 0, 4, NW)
            for j in range(2, DB):
                lo(j, 0, 4, NW)
                mem_lo(j)
            lo(4, 0, 4, NW)
            dve.wait_ge(ev("gains_turned"), 2)
            v.tensor_copy(gains[:, KD:N_ROWS], small[:, 1, 0:N_ROWS - KD]).then_inc(ev("gains"), 1)
            dve.wait_ge(ev("gains"), 2)
            for j in range(3):
                lo(5 + j, 0, 4, NW)
                x_lo(j)
            x_lo(3)
            ffn(1, "x1")

            def step_products(k):
                h, l = divmod(k, STEPS)
                if l == 0:
                    return
                m = 2 ** (l - 1)
                w = wave[:, k % 2, :].rearrange("p (n u m) -> p n u m", u=2, m=m)
                dve.wait_ge(ev("decays"), h * (STEPS - 1) + l)
                for u, src in ((1, qxT), (0, kxT)):
                    s = src[:].rearrange("p h t -> p (h t)").rearrange("p (n u m) -> p n u m", u=2, m=m)
                    ins = v.tensor_tensor(w[:, :, u, :], w[:, :, u, :], s[:, :, u, :], ALU.mult)
                ins.then_inc(ev("waves"), 1)

            def step_take(k):
                h, l = divmod(k, STEPS)
                for b in range(2):
                    dve.wait_ge(small_ready[b], fills["steps"] + k + 1)
                    src = small[:, b, :].rearrange("p (h t) -> p h t", h=HH)
                    if l == 0:
                        ins = v.tensor_tensor(AT[:, h * HH:(h + 1) * HH, b, :], src, under(ident[:], HH), ALU.mult)
                    elif l < LEVELS:
                        if b == 0:
                            dve.wait_ge(small_taken[1], k)
                        ins = v.copy_predicated(AT[:, h * HH:(h + 1) * HH, b, :], under(level_mask[:, l, :], HH), src)
                    else:
                        ins = v.tensor_copy(AT[:, h * HH + 2 * b:h * HH + 2 * b + 2, 2, :], src[:, 0:2, :])
                    ins.then_inc(small_taken[b], 1)

            def mixer(m):
                if m < 4:
                    entry("x2", m, M)
                for h, m0 in ((0, 6), (1, 30)):
                    if m == m0:
                        for b in range(2):
                            dve.wait_ge(tr_ready[b], groups[f"hf{h}"] + 1)
                            for i in range(2):
                                n = 2 * b + i
                                c = h * HH + n
                                ins = v.tensor_scalar(bT[:, n, :], tr[:, b, i * SEQ:(i + 1) * SEQ], bound[:, 1, c:c + 1], bound[:, 0, c:c + 1],
                                                      ALU.mult, ALU.add)
                            ins.then_inc(tr_taken[b], 1)
                        for b in range(2):
                            dve.wait_ge(tr_taken[b], groups[f"hf{h}"] + 1)
                        dve.sem_inc(ev("forget"), 1)
                    if m == m0 + 1:
                        dve.wait_ge(ev("log_forget"), h + 1)
                        dve.wait_ge(ev("complement"), h + 1)
                        for n in range(HH):
                            ins = v.tensor_tensor_scan(bT[:, n, :], one[:, 0:1].broadcast_to([P, SEQ]), lfT[:, n, :], 0.0, ALU.mult, ALU.add)
                        ins.then_inc(ev("running"), 1)
                if m == 14:
                    turned_lo(cqT_hi, cqT_lo, 0, groups["cq"], 0, splits["cq"], 0, gain=col["mla_q_a_norm"])
                if m == 18:
                    turned_lo(ckvT_hi, ckvT_lo, 0, groups["ckv"], 0, splits["ckv"], 0, gain=col["mla_kv_a_norm"], tiles=KR)
                for h in range(2):
                    if 0 <= m - STEP0[h] < STEPS:
                        step_products(h * STEPS + m - STEP0[h])
                    if 0 <= m - 2 - STEP0[h] < STEPS:
                        step_take(h * STEPS + m - 2 - STEP0[h])
                for b in range(2):
                    if m == 45 + b:
                        B = blocks["kv_up"] + 2 * b + 1
                        dve.wait_ge(ev("rsq_ckv"), 1)
                        dve.wait_ge(slot_used, slots["kv_up"] + b + 1)
                        for t in range(TT):
                            ins = v.tensor_scalar(kv_nat[:, t, (2 * b + 1) * NW:(2 * b + 2) * NW], acc[:, B % 2, t, :], cols(rsq, "ckv", t, 1),
                                                  None, ALU.mult)
                        ins.then_inc(acc_taken[B % 2], 1)

            done(v.memset(one[:], 1.0))
            done.wait()
            for m in range(40):
                lo(M + m, 0, 4, MIX_WIDTH[MIX[m // 4]])
                mixer(m)
            for m in range(40, 47):
                lo(M + m, 0, 4, NW)
                mixer(m)

            for t in range(TT):
                dve.wait_ge(ev("q_squares"), t + 1)
                src = (flat_stage, o_hg[:].rearrange("p a b -> p (a b)"))[t][:, 0:AH * QK]
                ins = v.tensor_reduce(cols(sums, "q", t * AH, AH), src.rearrange("p (h c) -> p h c", h=AH), AX, ALU.add)
                if t == 0:
                    done(ins)
            done.wait()
            ins.then_inc(ev("sums_q"), 1)
            kpe = ckv_nat[:, :, KR * P:KR * P + ROPE]
            done(v.tensor_tensor(k_rot[:], kpe, kpe, ALU.mult))
            done.wait()
            done(v.tensor_reduce(sums[:, KPE:KPE + TT], k_rot[:], AX, ALU.add))
            for t in range(TT):
                dve.wait_ge(ev("k_squares"), t + 1)
                done(v.tensor_reduce(cols(sums, "k", t * AH, AH), flat_stage[:, t * AH * P:(t + 1) * AH * P].rearrange("p (h c) -> p h c", h=AH),
                                     AX, ALU.add))
            done.wait()
            for t in range(TT):
                ins = v.tensor_scalar(cols(sums, "k", t * AH, AH), cols(sums, "k", t * AH, AH), sums[:, KPE + t:KPE + t + 1], None, ALU.add)
                if t == 0:
                    done(ins)
            done.wait()
            ins.then_inc(ev("sums_k"), 1)

            for h in range(2):
                for t in range(TT):
                    cols_h = slice(h * NW, (h + 1) * NW)
                    dve.wait_ge(ev("hg_squares"), 2 * h + t + 1)
                    v.tensor_tensor(o_hg[:, t, cols_h], small[:, t, :], G[:, t, cols_h], ALU.mult).then_inc(small_taken[t], 1)
                    done(v.tensor_reduce(cols(sums, "hg", t * HG + h * HH, HH), stage[:, 2 * h + t, :].rearrange("p (h c) -> p h c", h=HH), AX, ALU.add))
            done.wait()
            dve.sem_inc(ev("sums_hg"), 1)

            dve.wait_ge(ev("rsq_q"), 1)
            for t in range(TT):
                q = q_nat[:, t, :].rearrange("p (h c) -> p h c", h=AH)
                done(v.tensor_tensor(q, q, over(cols(rsq, "q", t * AH, AH), QK), ALU.mult))
            done.wait()
            dve.sem_inc(ev("q_scaled"), 1)
            dve.wait_ge(ev("rsq_k"), 1)
            for t in range(TT):
                k = kv_nat[:, t, :].rearrange("p (h c) -> p h c", h=AH)[:, :, 0:P]
                done(v.tensor_tensor(k, k, over(cols(rsq, "k", t * AH, AH), P), ALU.mult))
            done.wait()
            dve.sem_inc(ev("k_scaled"), 1)

            def rotate(dst, src, gain, t, n, c_tmp, s_tmp):
                done(v.tensor_tensor(dst, src, under(gain, n), ALU.mult))
                done.wait()
                d4 = dst.rearrange("p h (u f) -> p h u f", u=2)
                for tmp, k in ((c_tmp, 1), (s_tmp, 0)):
                    w = cs[:, k, t, :].unsqueeze(1).unsqueeze(1).broadcast_to([P, n, 2, RH])
                    done(v.tensor_tensor(tmp, d4, w, ALU.mult))
                done.wait()
                done(v.tensor_tensor(d4[:, :, 0, :], c_tmp[:, :, 0, :], s_tmp[:, :, 1, :], ALU.subtract))
                done(v.tensor_tensor(d4[:, :, 1, :], c_tmp[:, :, 1, :], s_tmp[:, :, 0, :], ALU.add))
                done.wait()

            tmp = [stage[:, i, :].rearrange("p (h u f) -> p h u f", u=2, f=RH) for i in range(2)]
            for t in range(TT):
                rotate(q_pe[:, t], q_nat[:, t, :].rearrange("p (h c) -> p h c", h=AH)[:, :, P:QK], pe_gain[:, 0, :], t, AH, tmp[0], tmp[1])
            dve.wait_ge(tr_ready[1], groups["qn"] + 2)
            for n in range(2):
                done(v.memset(qTp[n][(1 - n) * ROPE:(2 - n) * ROPE], 0.0))
            done.wait()
            dve.sem_inc(ev("q_rotated"), 1)
            for t in range(TT):
                rotate(k_rot[:, t:t + 1, :], kpe[:, t:t + 1, :], pe_gain[:, 1, :], t, 1, tmp[0][:, 0:1], tmp[1][:, 0:1])
                done(v.tensor_tensor(k_pe[:, t], under(k_rot[:, t, :], AH), over(cols(rsq, "k", t * AH, AH), ROPE), ALU.mult))
            done.wait()
            dve.sem_inc(ev("k_rotated"), 1)
            dve.wait_ge(ev("rsq_hg"), 1)
            for t in range(TT):
                o = o_hg[:, t, :].rearrange("p (h c) -> p h c", h=HG)
                done(v.tensor_tensor(o, o, over(cols(rsq, "hg", t * HG, HG), P), ALU.mult))
            done.wait()
            dve.sem_inc(ev("hg_scaled"), 1)
            for i in range(2):
                turned_lo(catT_hi, catT_lo, 8 + 4 * i, groups["cat_hg"] + i, 0, splits["cat_hg"] + i, 0, gain=col["hg_out_norm"], step=0)

            KEYS = (SEQ, P)

            def parts(p):
                base_ = (p % 2) * 1024
                return [flat_stage[:, base_ + 2 * SEQ * b:base_ + 2 * SEQ * b + 2 * KEYS[b]].rearrange("p (h k) -> p h k", h=2) for b in range(2)]

            score_fill, out_fill = FILL_ORDER
            def shift(p):
                for b, s in enumerate(parts(p)):
                    dve.wait_ge(small_ready[b], fills["mla"] + score_fill[p] + 1)
                    v.tensor_tensor(s, small[:, b, 0:2 * KEYS[b]].rearrange("p (h k) -> p h k", h=2), under(causal[:, SEQ - KEYS[b]:SEQ], 2),
                                    ALU.add).then_inc(small_taken[b], 1)
                for b, s in enumerate(parts(p)):
                    dve.wait_ge(small_taken[b], fills["mla"] + score_fill[p] + 1)
                    done(v.tensor_reduce(smax[:, p % 2, 2 * b:2 * b + 2], s, AX, ALU.max))
                done.wait()
                for b, s in enumerate(parts(p)):
                    done(v.tensor_tensor(s, s, over(smax[:, p % 2, 2 * b:2 * b + 2], KEYS[b]), ALU.subtract))
                done.wait()
                dve.sem_inc(ev("shifted"), 1)

            def outputs(p):
                dve.wait_ge(ev("exps"), p + 1)
                for b, s in enumerate(parts(p)):
                    done(v.tensor_reduce(ssum[:, p % 2, 2 * b:2 * b + 2], s, AX, ALU.add))
                done.wait()
                done(v.reciprocal(srec[:, p % 2, :], ssum[:, p % 2, :]))
                done.wait()
                for b in range(2):
                    dve.wait_ge(small_ready[b], fills["mla"] + out_fill[p] + 1)
                    v.tensor_tensor(o_mla[:, 1 - b, 2 * p * P:2 * (p + 1) * P].rearrange("p (h c) -> p h c", h=2),
                                    small[:, b, 0:2 * P].rearrange("p (h c) -> p h c", h=2), over(srec[:, p % 2, 2 * b:2 * b + 2], P),
                                    ALU.mult).then_inc(small_taken[b], 1)
                for b in range(2):
                    dve.wait_ge(small_taken[b], fills["mla"] + out_fill[p] + 1)
                dve.sem_inc(ev("o_mla"), 1)

            shift(0)
            for p in range(AH // 2):
                if p + 1 < AH // 2:
                    shift(p + 1)
                outputs(p)
            dve.wait_ge(ev("rsq_o_mla"), 1)
            for t in range(TT):
                done(v.tensor_scalar(o_mla[:, t, :], o_mla[:, t, :], cols(rsq, "o_mla", t, 1), None, ALU.mult))
            done.wait()
            dve.sem_inc(ev("o_scaled"), 1)
            for i in range(2):
                turned_lo(catT_hi, catT_lo, 4 * i, groups["cat_mla"] + i, 0, splits["cat_mla"] + i, 0, gain=col["mla_out_norm"])

            for j in range(DB):
                for s in range(4):
                    if j or s >= 2:
                        lo(slots["w_out"] + 4 * j + s, 0, 4, NW)
                    if j and s == 1:
                        add_block(blocks["w_out"] + j - 1, slots["w_out"] + 4 * j, j - 1, 1.0)
                    if j and s == 2:
                        turned_lo(hT_hi, hT_lo, 4 * (j - 1), groups["x_out"] + j - 1, 0, splits["x_out"] + j - 1, 0, gain=col["xattn_norm"])

            for s in range(4):
                lo(slots["xq"] + s, 0, 4, NW)
                entry("x3", s, slots["xq"])
            for s in range(2):
                lo(slots["w_o"] + s, 0, 4, NW)
            dve.wait_ge(ev("xq_squares"), 1)
            v.tensor_reduce(cols(sums, "xq"), nat.rearrange("p t (h c) -> p (t h) c", h=XH), AX, ALU.add).then_inc(ev("sums_xq"), 1)
            dve.wait_ge(ev("rsq_xq"), 1)
            q = gate.rearrange("p t (h c) -> p (t h) c", h=XH)
            v.tensor_tensor(q, q, over(cols(rsq, "xq"), P), ALU.mult).then_inc(ev("xq_scaled"), 1)
            for p in range(XH // 2):
                for t in range(TT):
                    dve.wait_ge(small_ready[t], fills["xattn"] + p + 1)
                    done(v.tensor_reduce(smax[:, p, 2 * t:2 * t + 2], small[:, t, :].rearrange("p (h k) -> p h k", h=2), AX, ALU.max))
                done.wait()
                for t in range(TT):
                    v.tensor_tensor(stage[:, 2 * p + t, :].rearrange("p (h k) -> p h k", h=2), small[:, t, :].rearrange("p (h k) -> p h k", h=2),
                                    over(smax[:, p, 2 * t:2 * t + 2], MEM), ALU.subtract).then_inc(small_taken[t], 1)
                for t in range(TT):
                    dve.wait_ge(small_taken[t], fills["xattn"] + p + 1)
                dve.sem_inc(ev("x_shifted"), 1)
            for p in range(XH // 2):
                dve.wait_ge(ev("x_exps"), p + 1)
                done(v.tensor_reduce(ssum[:, p, :], stage[:, 2 * p:2 * p + 2, :].rearrange("p t (h k) -> p (t h) k", h=2), AX, ALU.add))
                done.wait()
                done(v.reciprocal(srec[:, p, :], ssum[:, p, :]))
                done.wait()
            for p in range(XH // 2):
                for t in range(TT):
                    dve.wait_ge(small_ready[t], fills["xattn"] + XH // 2 + p + 1)
                    v.tensor_tensor(xo[:, t, 2 * p * P:2 * (p + 1) * P].rearrange("p (h c) -> p h c", h=2),
                                    small[:, t, 0:2 * P].rearrange("p (h c) -> p h c", h=2), over(srec[:, p, 2 * t:2 * t + 2], P),
                                    ALU.mult).then_inc(small_taken[t], 1)
            turned_lo(xoT_hi, xoT_lo, 0, groups["xo"], 0, splits["xo"], 0)
            for j in range(2, DB):
                lo(slots["w_o"] + j, 0, 4, NW)
                add_block(blocks["w_o"] + j - 2, slots["w_o"] + j - 1, j - 2, 1.0)
            turned_lo(hT_hi, hT_lo, 0, groups["x_o"], 0, splits["x_o"], 0, gain=col["ffn2_norm"])
            lo(slots[2, "up", 0], 0, 4, NW)
            add_block(blocks["w_o"] + DB - 2, slots["w_o"] + DB - 1, DB - 2, 1.0)
            for j in range(1, DB - 1):
                turned_lo(hT_hi, hT_lo, 4 * j, groups["x_o"] + j, 0, splits["x_o"] + j, 0, gain=col["ffn2_norm"])
            ffn(2, "x4")
            add_block(blocks[2, "down", 1] + DB - 1, slots[2, "down", 1] + 8 * DB, DB - 1, 0.5)

        @block.tensor
        def _(pe):
            mm = nc.tensor.matmul

            def turn(g, rep, srcs):
                for b in range(2):
                    if g:
                        pe.wait_ge(tr_taken[b], g + rep)
                    for n, s in enumerate(srcs[b]):
                        ins = nc.tensor.transpose(tr[:, b, n * P:(n + 1) * P], s, ident[:])
                    ins.then_inc(tr_ready[b], 1)

            def turn_features(g, rep, part, tiles=4):
                h = -(-tiles // 2)
                turn(g, rep, [[part(m, t) for m in ms for t in range(TT)] for ms in (range(h), range(h, tiles))])

            def of(src, col0=0):
                return lambda m, t: src[:, t, col0 + m * P:col0 + (m + 1) * P]

            def slot(c, rep, B, lhs_hi, lhs_lo, k0, tiles, width, first, last, off=0, full=None, signal=True):
                pe.wait_ge(lo_done, c + rep + 1)
                full = full or width
                for kk in range(tiles):
                    w0 = kk * full + off
                    wh, wl = w_hi[:, c % SPLIT, w0:w0 + width], w_lo[:, c % SPLIT, w0:w0 + width]
                    for t in range(TT):
                        dst = acc[:, B % 2, t, 0:width]
                        xh = lhs_hi[:, k0 + kk, t * P:(t + 1) * P]
                        xl = lhs_lo[:, k0 + kk, t * P:(t + 1) * P]
                        mm(dst, xh, wh, start=first and kk == 0, stop=False)
                        mm(dst, xl, wh, start=False, stop=False)
                        ins = mm(dst, xh, wl, start=False, stop=last and kk == tiles - 1)
                if signal:
                    ins.then_inc(slot_used, 1)

            def free(B, k=0, i=0):
                if B + 2 * k >= 2:
                    pe.wait_ge(acc_taken[B % 2], B // 2 + k + i)

            def stands(B):
                pe.wait_ge(acc_taken[B % 2], B // 2 + 1)

            def split_stands(g):
                for b in range(2):
                    pe.wait_ge(tr_taken[b], g + 1)

            def entry(name, s):
                g = groups[ENTRY[name][0]] + DB - 1
                if s == 1:
                    stands(LAST_BLOCK[name])
                    turn_features(g, 0, of(x, (DB - 1) * NW))
                if s == 2:
                    split_stands(g)

            def fill(f):
                if f:
                    for b in range(2):
                        pe.wait_ge(small_taken[b], f)

            def ffn(f, name):
                for h, (f0, tiles) in enumerate(HALVES):
                    c0, b0, g0 = slots[f, "up", h], blocks[f, "up", h], groups[f, "up", h]
                    full = tiles // 4

                    def pair(i, k, width=NW):
                        c, rep, prev = c0 + 8 * k, 8 * i, k > 0
                        for b in range(2):
                            B = b0 + b
                            free(B, k, i)
                            for s in range(4):
                                slot(c + 4 * b + s, rep, B, hT_hi, hT_lo, 4 * s, 4, width, s == 0, s == 3)
                                if prev and b == 0 and s == 1:
                                    pe.wait_ge(acc_taken[(b0 + 1) % 2], (b0 + 1) // 2 + k + i)
                                    turn_features(g0 + k - 1, i, of(nat))
                                if not prev and b == 0 and h == 0 and f == 2:
                                    entry(name, s)
                                if not prev and b == 1 and h == 0 and f == 1 and s == 0:
                                    pe.wait_ge(ev("memk"), 1)
                                    turn_features(groups["memk"], 0, lambda m, t: memk[:, ((m // 2) * MT + t) * 2 + m % 2, :])

                    pair(0, 0)
                    with pe.Fori(0, full - 1) as i:
                        pair(i, 1)
                    last = full - 1
                    if tiles % 4:
                        last = full
                        pair(0, full, (tiles % 4) * P)
                    cd, bd = slots[f, "down", h], blocks[f, "down", h]
                    ns = down_tiles(tiles)
                    for j in range(DB):
                        B = bd + j
                        free(B)
                        k = 0
                        for s in range(8):
                            if j == 0 and s == 6:
                                split_stands(g0 + last)
                            slot(cd + 8 * j + s, 0, B, actT_hi, actT_lo, k, ns[s], NW, s == 0, s == 7)
                            k += ns[s]
                            if j == 0 and s == 1:
                                pe.wait_ge(acc_taken[(b0 + 1) % 2], (b0 + 1) // 2 + last + 1)
                                turn_features(g0 + last, 0, of(nat), tiles - 4 * last)
                            if j > 0 and s == 2 and h == 1 and f == 1:
                                stands(B - 1)
                                turn_features(groups[f, "down", h] + j - 1, 0, of(x, (j - 1) * NW))

            def turn_mem(j):
                pe.wait_ge(mem_in[j], 16)
                turn_features(groups["mem"] + j, 0, of(mem_nat, j * NW))

            pe.wait_ge(mem_rows_in, 16 * 2)
            nc.tensor.transpose(small[:, 0, 0:KD], mem_rows[0:KD, :], ident[0:KD, 0:KD]).then_inc(ev("gains_turned"), 1)
            turn_mem(0)
            turn_mem(1)
            for b in range(2):
                for s in range(4):
                    if b == 0:
                        split_stands(groups["mem"] + s)
                    slot(4 * b + s, 0, b, mT_hi, mT_lo, 4 * s, 4, NW, s == 0, s == 3)
                    if b == 0 and s < 2:
                        turn_mem(2 + s)
                    if b == 0 and s == 2:
                        pe.wait_ge(rows_in, 16 * (len(GAIN_ROWS) - 1))
                        R = N_ROWS - KD
                        nc.tensor.transpose(small[:, 1, 0:R], rows[0:R, :], ident[0:R, 0:R]).then_inc(ev("gains_turned"), 1)
                    if 3 <= 4 * b + s < 3 + DB:
                        j = 4 * b + s - 3
                        if j == 0:
                            pe.wait_ge(x_in, 16 * TT)
                        turn_features(groups["x"] + j, 0, of(x, j * NW))
            split_stands(groups["x"] + DB - 1)
            ffn(1, "x1")

            def step(k):
                h, l = divmod(k, STEPS)
                fill(fills["steps"] + k)
                if l == 0:
                    pe.wait_ge(ev("complement"), h + 1)
                    split_stands(groups[f"hq{h}"])
                else:
                    pe.wait_ge(ev("waves"), h * (STEPS - 1) + l)
                w = wave[:, k % 2, :].rearrange("p (h t) -> p h t", h=HH)
                for b in range(2):
                    for n in range(HH if l < LEVELS else HH // 2):
                        if l == 0:
                            keys, queries = kxT[:, n, b * P:(b + 1) * P], qxT[:, n, b * P:(b + 1) * P]
                        elif l < LEVELS:
                            keys = queries = w[:, n, b * P:(b + 1) * P]
                        else:
                            keys, queries = w[:, 2 * b + n, 0:P], w[:, 2 * b + n, P:2 * P]
                        ins = mm(small[:, b, n * P:(n + 1) * P], keys, queries, start=True, stop=True)
                    ins.then_inc(small_ready[b], 1)

            def mixer(m):
                if m < 4:
                    entry("x2", m)
                if m % 4 == 0 and m:
                    b = m // 4 - 1
                    n = MIX[b] if b < len(MIX) else ""
                    if n in groups:
                        stands(blocks["mix"] + b)
                        src, tiles = {"hf": (gate, 4), "hq": (nat, 4), "cq": (gate, QR), "ck": (ckv_nat, KR)}[n[:2]]
                        turn_features(groups[n], 0, of(src), tiles)
                for h in range(2):
                    if 0 <= m - STEP0[h] < STEPS:
                        step(h * STEPS + m - STEP0[h])

            for m in range(40):
                B = blocks["mix"] + m // 4
                if m % 4 == 0:
                    free(B)
                slot(M + m, 0, B, hT_hi, hT_lo, 4 * (m % 4), 4, MIX_WIDTH[MIX[m // 4]], m % 4 == 0, m % 4 == 3)
                mixer(m)
            for b in range(3):
                if b == 0:
                    split_stands(groups["cq"])
                free(blocks["q_up"] + b)
                slot(slots["q_up"] + b, 0, blocks["q_up"] + b, cqT_hi, cqT_lo, 0, QR, NW, True, True)
                mixer(40 + b)
            for b in range(2):
                if b == 0:
                    split_stands(groups["ckv"])
                for n in range(2):
                    B = blocks["kv_up"] + 2 * b + n
                    free(B)
                    slot(slots["kv_up"] + b, 0, B, ckvT_hi, ckvT_lo, 0, KR, NW, True, True, off=n * NW, full=2 * NW, signal=n == 1)
                mixer(43 + b)

            for h in range(2):
                f = fills["av"] + h
                fill(f)
                for t in range(TT):
                    for n in range(HH):
                        head = h * HH + n
                        dst = small[:, t, n * P:(n + 1) * P]
                        v = slice(head * P, (head + 1) * P)
                        ins = mm(dst, AT[:, head, t, :], V[:, t, v], start=True, stop=t == 0)
                        if t == 1:
                            ins = mm(dst, AT[:, head, 2, :], V[:, 0, v], start=False, stop=True)
                    ins.then_inc(small_ready[t], 1)

            pe.wait_ge(ev("q_scaled"), 1)
            for i in range(2):
                turn_features(groups["qn"] + i, 0, lambda m, t: q_nat[:, t, (4 * i + m) * QK:(4 * i + m) * QK + P])
            pe.wait_ge(ev("k_scaled"), 1)
            for i in range(2):
                turn_features(groups["kn"] + i, 0, lambda m, t: kv_nat[:, t, (4 * i + m) * 2 * P:(4 * i + m) * 2 * P + P])
            pe.wait_ge(ev("q_rotated"), 1)
            turn_features(groups["qp"], 0, lambda m, t: q_pe[:, t, 2 * m:2 * m + 2, :].rearrange("p h c -> p (h c)"))
            pe.wait_ge(ev("k_rotated"), 1)
            turn_features(groups["kp"], 0, lambda m, t: k_pe[:, t, 2 * m:2 * m + 2, :].rearrange("p h c -> p (h c)"))
            pe.wait_ge(ev("hg_scaled"), 1)
            for i in range(2):
                turn_features(groups["cat_hg"] + i, 0, of(o_hg, i * NW))

            score_fill, out_fill = FILL_ORDER

            def scores(p):
                f = fills["mla"] + score_fill[p]
                fill(f)
                for b, (t, keys) in enumerate(((1, SEQ), (0, P))):
                    for n in range(2):
                        h = 2 * p + n
                        dst = small[:, b, n * keys:(n + 1) * keys]
                        mm(dst, qTn[:, h, t * P:(t + 1) * P], kTn[:, h, 0:keys], start=True, stop=False)
                        ins = mm(dst, qTp[n][:, p, t * P:(t + 1) * P], kTp[:, p, 0:keys], start=False, stop=True)
                    ins.then_inc(small_ready[b], 1)

            def probs(p):
                s = flat_stage[:, (p % 2) * 1024:(p % 2) * 1024 + 6 * P]
                pe.wait_ge(ev("exps"), p + 1)
                turn(groups["prob"] + p, 0, [[s[:, n * P:(n + 1) * P] for n in ns] for ns in (range(4), range(4, 6))])

            def outputs(p):
                f = fills["mla"] + out_fill[p]
                fill(f)
                split_stands(groups["prob"] + p)
                pT = probT[:, p % 2, :]
                for b in range(2):
                    for n in range(2):
                        h = 2 * p + n
                        dst = small[:, b, n * P:(n + 1) * P]
                        for k in range(2 - b):
                            c = (2 * n + k) * P if b == 0 else (4 + n) * P
                            ins = mm(dst, pT[:, c:c + P], kv_nat[:, k, h * 2 * P + P:(h + 1) * 2 * P], start=k == 0, stop=k == 1 - b)
                    ins.then_inc(small_ready[b], 1)

            flat_stage = stage[:].rearrange("p a b -> p (a b)")
            split_stands(groups["kp"])
            scores(0)
            for p in range(AH // 2):
                if p + 1 < AH // 2:
                    scores(p + 1)
                probs(p)
                outputs(p)

            split_stands(groups["cat_hg"] + 1)
            for j in range(DB):
                B = blocks["w_out"] + j
                free(B)
                for s, k in enumerate((8, 12, 0, 4)):
                    if j == 0 and s == 2:
                        pe.wait_ge(ev("o_scaled"), 1)
                        for i in range(2):
                            turn_features(groups["cat_mla"] + i, 0, of(o_mla, i * NW))
                        split_stands(groups["cat_mla"] + 1)
                    slot(slots["w_out"] + 4 * j + s, 0, B, catT_hi, catT_lo, k, 4, NW, s == 0, s == 3)
                    if j and s == 1:
                        stands(B - 1)
                        turn_features(groups["x_out"] + j - 1, 0, of(x, (j - 1) * NW))

            B = blocks["xq"]
            free(B)
            for s in range(4):
                slot(slots["xq"] + s, 0, B, hT_hi, hT_lo, 4 * s, 4, NW, s == 0, s == 3)
                entry("x3", s)
            pe.wait_ge(ev("xq_scaled"), 1)
            turn_features(groups["xq"], 0, of(gate))
            split_stands(groups["xq"])
            for p in range(XH // 2):
                fill(fills["xattn"] + p)
                for t in range(TT):
                    for n in range(2):
                        ins = mm(small[:, t, n * MEM:(n + 1) * MEM], xqT[:, 2 * p + n, t * P:(t + 1) * P], memkT[:, 2 * p + n, :], start=True, stop=True)
                    ins.then_inc(small_ready[t], 1)
            for p in range(XH // 2):
                pe.wait_ge(ev("x_exps"), p + 1)
                turn(groups["x_prob"] + p, 0, [[stage[:, 2 * p + t, n * P:(n + 1) * P] for n in range(4)] for t in range(TT)])
            for p in range(XH // 2):
                fill(fills["xattn"] + XH // 2 + p)
                split_stands(groups["x_prob"] + p)
                for t in range(TT):
                    for n in range(2):
                        for k in range(MT):
                            c = (2 * n + k) * P
                            ins = mm(small[:, t, n * P:(n + 1) * P], x_probT[:, p, t, c:c + P],
                                     memv[:, k, (2 * p + n) * P:(2 * p + n + 1) * P], start=k == 0, stop=k == MT - 1)
                    ins.then_inc(small_ready[t], 1)
            for t in range(TT):
                pe.wait_ge(small_taken[t], fills["xattn"] + XH)
            turn_features(groups["xo"], 0, of(xo))
            split_stands(groups["xo"])
            for j in range(DB):
                B = blocks["w_o"] + j
                free(B)
                slot(slots["w_o"] + j, 0, B, xoT_hi, xoT_lo, 0, 4, NW, True, True)
                if j >= 2:
                    stands(B - 2)
                    turn_features(groups["x_o"] + j - 2, 0, of(x, (j - 2) * NW))
            stands(blocks["w_o"] + DB - 2)
            turn_features(groups["x_o"] + DB - 2, 0, of(x, (DB - 2) * NW))
            ffn(2, "x4")


_INS = ["x", "mem", "positions", "ffn1_norm", "ffn1_w_gate", "ffn1_w_up", "ffn1_w_down", "mix_norm", "w_in", "mla_q_a_norm", "mla_w_q_up",
        "mla_kv_a_norm", "mla_w_kv_up", "mla_q_norm", "mla_k_norm", "mla_out_norm", "hg_lb_logits", "hg_out_norm", "w_out", "xattn_norm",
        "mem_norm", "xattn_w_q", "xattn_w_kv", "xattn_q_norm", "xattn_k_norm", "xattn_w_o", "ffn2_norm", "ffn2_w_gate", "ffn2_w_up",
        "ffn2_w_down"]


def constants():
    s, t = np.arange(P)[:, None], np.arange(P)[None, :]
    level_mask = np.zeros((P, LEVELS, P), np.int32)
    for level in range(1, LEVELS):
        m = 2 ** (level - 1)
        level_mask[:, level, :] = (s // (2 * m) == t // (2 * m)) & (s // m % 2 == 0) & (t // m % 2 == 1)
    causal = np.zeros((P, 2 * P), np.float32)
    causal[:, P:] = np.where(t <= s, 0.0, -1e30)
    freq = np.float32(10000.0) ** (-np.arange(RH, dtype=np.float32) / np.float32(RH))
    return {"ident": np.eye(P, dtype=np.float32), "level_mask": level_mask, "causal": causal,
            "freq": np.ascontiguousarray(np.broadcast_to(freq.astype(np.float32), (P, RH)))}


def kernel(**inputs):
    import concourse.bacc as bacc
    from concourse.bass_utils import run_bass_kernel_spmd

    nc = bacc.Bacc("TRN2", target_bir_lowering=False, num_devices=1)
    data = {n: np.ascontiguousarray(inputs[n]) for n in _INS}
    data.update(constants())
    arrays, args = {}, {}
    for n, v in data.items():
        arrays[f"in_{n}"] = v
        args[n] = nc.dram_tensor(f"in_{n}", v.shape, mybir.dt.from_np(v.dtype), kind="ExternalInput").ap()
    out = nc.dram_tensor("out_0", data["x"].shape, F32, kind="ExternalOutput").ap()
    layer(nc, args, out)
    r = run_bass_kernel_spmd(nc, [arrays], core_ids=[0])
    return r.results[0]["out_0"]
```

```python
from contextlib import ExitStack

import numpy as np

import concourse.bass as bass
from concourse import mybir

F32 = mybir.dt.float32
F32R = mybir.dt.float32r
I32 = mybir.dt.int32
U8 = mybir.dt.uint8
ALU = mybir.AluOpType
ACT = mybir.ActivationFunctionType
AX = mybir.AxisListType.X

P = 128
NW = 512
RAW = 4
SPLIT = 2
EPS = 1e-6
RH = 32
HALF = P // 2
LEVELS = 8
TWO_PI = 2 * np.pi
PI_1 = 6.28125
PI_2 = float(np.float32(round((TWO_PI - PI_1) * 2 ** 20) / 2 ** 20))
PI_3 = TWO_PI - PI_1 - PI_2
ROUND = 1.5 * 2 ** 23


class Done:

    def __init__(self, eng, sem):
        self.eng, self.sem, self.n = eng, sem, 0

    def __call__(self, ins):
        ins.then_inc(self.sem, 1)
        self.n += 1

    def wait(self):
        if self.n:
            self.eng.wait_ge(self.sem, self.n)


def down_tiles(tiles):
    return [min(4, tiles - k) for k in range(0, tiles, 4)]


def over(ap, n):
    return ap.unsqueeze(2).broadcast_to([ap.shape[0], ap.shape[1], n])


def under(ap, n):
    return ap.unsqueeze(1).broadcast_to([ap.shape[0], n, ap.shape[1]])


def uppers(ap, level):
    return ap.rearrange("p (n u m) -> p n u m", u=2, m=2 ** (level - 1))[:, :, 1, :]


def layer(nc, a, out):
    SEQ, D = a["x"].shape[1:]
    MEM = a["mem"].shape[1]
    FF = a["ffn1_w_gate"].shape[2]
    TT, MT = SEQ // P, MEM // P
    KD, DB = D // P, D // NW
    FT, FA = FF // P, 24
    HALVES = ((0, FA), (FA, FT - FA))
    ROPE = 2 * RH
    QR = a["mla_q_a_norm"].shape[1] // P
    KR = a["mla_kv_a_norm"].shape[1] // P
    QK = a["mla_q_norm"].shape[1]
    AH = a["mla_w_q_up"].shape[2] // QK
    HG = a["hg_lb_logits"].shape[1] // P
    HH = HG // 2
    XH = a["xattn_w_o"].shape[1] // P
    SCALE, X_SCALE = float(QK) ** -0.5, float(P) ** -0.5

    ctx = ExitStack()
    with ctx:
        def sb(name, shape, dt=F32):
            return ctx.enter_context(nc.sbuf_tensor(name, shape, dt))

        def sem(name):
            return ctx.enter_context(nc.semaphore(name))

        x = sb("x_res", [P, TT, D])
        raw = sb("w_raw", [P, RAW, 4 * NW])
        w_hi = sb("w_hi", [P, SPLIT, 4 * NW], F32R)
        w_lo = sb("w_lo", [P, SPLIT, 4 * NW], F32R)
        stage = sb("stage", [P, 2 * TT, NW])
        gate, nat = stage[:, 0:TT, :], stage[:, TT:2 * TT, :]
        memkT = sb("memkT", [P, XH, MEM])
        memv = sb("memv", [P, MT, XH * P])
        ident = sb("ident", [P, P])
        gains = sb("gains", [P, 116])
        level_mask = sb("level_mask", [P, LEVELS, P], U8)
        causal = sb("causal", [P, SEQ])
        one = sb("one", [P, 1])
        cs = sb("cos_sin", [P, 2, TT, RH])
        pe_gain = sb("pe_gain", [P, 2, ROPE])
        bound = sb("bound", [P, 2, HG])
        sums = sb("sums", [P, 82])
        rsq = sb("rsq", [P, 82])
        half = sb("minus_half", [P, 16])
        smax = sb("score_max", [P, 4, 4])
        ssum = sb("score_sum", [P, 4, 4])
        srec = sb("score_rec", [P, 4, 4])

        KB = 1024
        slab_bytes = 106 * KB + 512
        base = -(-nc.sbuf_base // 64) * 64
        sb("slab_fence", [P, (slab_bytes + base - nc.sbuf_base) // 4])

        def at(name, kb, shape, dt=F32):
            n = 4
            for v in shape[1:]:
                n *= v
            assert kb * KB + n <= slab_bytes, name
            return nc.alloc_sbuf_tensor_at(name, shape, dt, offset=base + int(kb * KB))

        hT_hi = at("hT_hi", 0, [P, KD, SEQ], F32R)
        hT_lo = at("hT_lo", 16, [P, KD, SEQ], F32R)
        q_nat = at("q_nat", 0, [P, TT, AH * QK])
        kv_nat = at("kv_nat", 12, [P, TT, AH * 2 * P])
        q_pe = at("q_pe", 28, [P, TT, AH, ROPE])
        probT = at("probT", 0, [P, 2, 6 * P])
        A0 = 32
        actT_hi = at("actT_hi", A0, [P, FA, SEQ], F32R)
        actT_lo = at("actT_lo", A0 + 24, [P, FA, SEQ], F32R)
        mT_hi, mT_lo = actT_hi, actT_lo
        mem_nat = at("mem_nat", A0 + 48, [P, MT, D])
        memkv = at("memkv", A0 + 48, [P, 2 * MT, NW])
        memk = at("memk", A0 + 56, [P, 4 * MT, P])
        mem_rows = at("mem_gain_rows", A0 + 64, [P, P])
        rows = at("gain_rows", A0 + 64.5, [P, P])
        pos_i = at("pos_i", A0 + 65, [P, TT], I32)
        pos_f = at("pos_f", A0 + 65.0625, [P, TT])
        freq = at("freq", A0 + 65.125, [P, RH])
        ang = at("ang", A0 + 65.5, [P, 2, TT * RH])
        turns = at("turns", A0 + 66, [P, 2, TT * RH])
        rest = at("rest", A0 + 66.5, [P, 2, TT * RH])
        lbt = at("lbt", A0 + 67, [P, 6, HG])
        mask_i = at("mask_i", A0 + 68, [P, LEVELS, P], I32)
        bT = at("bT", A0, [P, 4, SEQ])
        kxT = at("kxT", A0 + 4, [P, 4, SEQ])
        qxT = at("qxT", A0 + 8, [P, 4, SEQ])
        lfT = at("lfT", A0 + 12, [P, 4, SEQ])
        wave = at("wave", A0 + 16, [P, 2, 4 * SEQ])
        AT = at("AT", A0 + 24, [P, HG, 3, P])
        V = at("V", A0 + 36, [P, TT, HG * P])
        G = at("G", A0 + 44, [P, TT, HG * P])
        cqT_hi = at("cqT_hi", A0 + 52, [P, QR, SEQ], F32R)
        cqT_lo = at("cqT_lo", A0 + 56, [P, QR, SEQ], F32R)
        ckvT_hi = at("ckvT_hi", A0 + 60, [P, KR, SEQ], F32R)
        ckvT_lo = at("ckvT_lo", A0 + 62, [P, KR, SEQ], F32R)
        ckv_nat = at("ckv_nat", A0 + 64, [P, TT, KR * P + ROPE])
        o_hg = at("o_hg", A0 + 66.5, [P, TT, HG * P])
        qTn = at("qTn", A0, [P, AH, SEQ])
        kTn = at("kTn", A0 + 8, [P, AH, SEQ])
        qTp = [at("qTp_even", A0 + 16, [P, AH // 2, SEQ]), at("qTp_odd", 6, [P, AH // 2, SEQ])]
        kTp = at("kTp", A0 + 20, [P, AH // 2, SEQ])
        k_pe = at("k_pe", A0 + 56, [P, TT, AH, ROPE])
        q_tmp = at("q_tmp", A0 + 12, [P, 2, AH, ROPE])
        k_tmp = at("k_tmp", A0 + 66.5, [P, 2, ROPE])
        k_sq = at("k_sq", A0 + 67.5, [P, TT, ROPE])
        o_mla = at("o_mla", A0 + 56, [P, TT, AH * P])
        catT_hi = at("catT_hi", A0 + 24, [P, 16, SEQ], F32R)
        catT_lo = at("catT_lo", A0 + 40, [P, 16, SEQ], F32R)
        xqT = at("xqT", A0, [P, XH, SEQ])
        x_probT = at("x_probT", A0 + 4, [P, 2, TT, 4 * P])
        xo = at("xo", A0 + 12, [P, TT, XH * P])
        xoT_hi = at("xoT_hi", A0 + 16, [P, XH, SEQ], F32R)
        xoT_lo = at("xoT_lo", A0 + 20, [P, XH, SEQ], F32R)

        acc = ctx.enter_context(nc.psum_tensor("acc", [P, 2, TT, NW], F32))
        tr = ctx.enter_context(nc.psum_tensor("tr", [P, 2, NW], F32))
        small = ctx.enter_context(nc.psum_tensor("small", [P, 2, NW], F32))


        loaded = [sem(f"raw_loaded{s}") for s in range(RAW)]
        hi_done = sem("hi_done")
        lo_done = sem("lo_done")
        slot_used = sem("slot_used")
        acc_taken = [sem("acc_taken0"), sem("acc_taken1")]
        tr_ready = [sem("tr_ready0"), sem("tr_ready1")]
        tr_taken = [sem("tr_taken0"), sem("tr_taken1")]
        t_hi = sem("turned_hi")
        small_ready = [sem("small_ready0"), sem("small_ready1")]
        small_taken = [sem("small_taken0"), sem("small_taken1")]
        dve_done, act_done, pool_done = sem("dve_done"), sem("act_done"), sem("pool_done")
        mem_rows_in, rows_in, const_in, x_in = sem("mem_gain_rows_in"), sem("gain_rows_in"), sem("const_in"), sem("x_in")
        mem_in = [sem(f"mem_in{j}") for j in range(D // NW)]
        out_done = sem("out_done")
        named = {}

        def ev(name):
            if name not in named:
                named[name] = sem(name)
            return named[name]

        GAIN_ROWS = [("mem_norm", KD), ("ffn1_norm", KD), ("mix_norm", KD), ("xattn_norm", KD), ("ffn2_norm", KD),
                     ("mla_out_norm", AH), ("hg_lb_logits", 2 * HG), ("mla_q_a_norm", QR), ("mla_kv_a_norm", KR),
                     ("xattn_q_norm", 1), ("xattn_k_norm", 1), ("hg_out_norm", 1), ("mla_q_norm", 1), ("mla_k_norm", 1)]
        col, N_ROWS = {}, 0
        for name, n in GAIN_ROWS:
            col[name] = N_ROWS
            N_ROWS += n

        NORMS = {"mem": (MT, D), "x1": (TT, D), "memk": (2 * MT * 2, P), "x2": (TT, D), "cq": (TT, QR * P), "ckv": (TT, KR * P),
                 "q": (TT * AH, QK), "k": (TT * AH, QK), "hg": (TT * HG, P), "o_mla": (TT, AH * P), "x3": (TT, D),
                 "xq": (TT * XH, P), "x4": (TT, D)}
        at_col, c = {}, 0
        for name, (n, _) in NORMS.items():
            at_col[name] = c
            c += n
        KPE = c

        def cols(t, name, i=0, n=None):
            c = at_col[name] + i
            return t[:, c:c + (NORMS[name][0] if n is None else n)]

        slots, blocks, groups, splits, fills = {}, {}, {}, {}, {}
        count = {}

        def number(table, name, n=1):
            table[name] = count.get(id(table), 0)
            count[id(table)] = table[name] + n

        def number_ffn(f):
            for h in range(2):
                pairs = -(-HALVES[h][1] // 4)
                number(slots, (f, "up", h), 8 * pairs)
                number(blocks, (f, "up", h), 2 * pairs)
                number(groups, (f, "up", h), pairs)
                number(splits, (f, "up", h), pairs)
                number(slots, (f, "down", h), len(down_tiles(HALVES[h][1])) * DB)
                number(blocks, (f, "down", h), DB)
                if h == 1 and f == 1:
                    number(groups, (f, "down", h), DB)
                    number(splits, (f, "down", h), DB)

        MIX = ["hf0", "hq0", "cq", "ckv", "hi0", "hf1", "hq1", "hg0", "hi1", "hg1"]
        STEPS = LEVELS + 1
        STEP0 = {0: 11, 1: 31}

        number(groups, "mem", DB)
        number(splits, "mem", DB)
        number(slots, "memkv", 8)
        number(blocks, "memkv", 2)
        number(groups, "x", DB)
        number(splits, "x", DB)
        number(groups, "memk")
        number_ffn(1)
        number(slots, "mix", 4 * len(MIX))
        number(blocks, "mix", len(MIX))
        for n in ("hf0", "hq0", "cq", "ckv", "hf1", "hq1"):
            number(groups, n)
        for n in ("cq", "ckv"):
            number(splits, n)
        number(slots, "q_up", 3)
        number(blocks, "q_up", 3)
        number(slots, "kv_up", 2)
        number(blocks, "kv_up", 4)
        number(fills, "steps", 2 * STEPS)
        number(fills, "av", 2)
        for n in ("cat_hg", "qn", "kn"):
            number(groups, n, 2)
        for n in ("qp", "kp"):
            number(groups, n)
        number(splits, "cat_hg", 2)
        number(fills, "mla", 2 * (AH // 2))
        number(groups, "prob", AH // 2)
        for n in ("w_out_hg", "w_out"):
            number(slots, n, 2 * DB)
            number(blocks, n, DB)
        number(groups, "cat_mla", 2)
        number(splits, "cat_mla", 2)
        number(groups, "x_out", DB)
        number(splits, "x_out", DB)
        number(slots, "xq", 4)
        number(blocks, "xq", 1)
        number(groups, "xq")
        number(fills, "xattn", 2 * (XH // 2))
        number(groups, "x_prob", XH // 2)
        number(groups, "xo")
        number(splits, "xo")
        number(slots, "w_o", DB)
        number(blocks, "w_o", DB)
        number(groups, "x_o", DB)
        number(splits, "x_o", DB)
        number_ffn(2)
        M = slots["mix"]
        FILL_ORDER = ([0, 1, 2, 4], [3, 5, 6, 7])

        ENTRY = {"x2": ((1, "down", 1), "mix_norm"), "x3": ("x_out", "xattn_norm"), "x4": ("x_o", "ffn2_norm")}
        LAST_BLOCK = {"x2": blocks[1, "down", 1] + DB - 1, "x3": blocks["w_out"] + DB - 1, "x4": blocks["w_o"] + DB - 1}
        FACTOR = {"x2": 0.5, "x3": 1.0, "x4": 1.0}
        MIX_WIDTH = {n: NW for n in MIX}
        MIX_WIDTH["ckv"] = KR * P + ROPE
        starts = {"cq": 0, "ckv": QR * P}
        q0 = QR * P + KR * P + ROPE
        for i, n in enumerate(("hq", "hf", "hi", "hg")):
            for h in range(2):
                starts[f"{n}{h}"] = q0 + (2 * i + h) * NW

        block = ctx.enter_context(nc.Block())

        @block.sync
        def _(sp):
            def load(c, rep, src, tiles, width):
                if c >= RAW:
                    sp.wait_ge(lo_done, c + rep - RAW + 1)
                dst = raw[:, c % RAW, 0:tiles * width].rearrange("p (k n) -> p k n", k=tiles)
                sp.dma_start(dst, src).then_inc(loaded[c % RAW], 16)

            def rows_of(w, k0, tiles, cols):
                return w[k0 * P:(k0 + tiles) * P, cols].rearrange("(k p) n -> p k n", p=P)

            def load_ffn(f):
                wg, wu, wd = (a[f"ffn{f}_w_{n}"][0] for n in ("gate", "up", "down"))
                for h, (f0, tiles) in enumerate(HALVES):
                    c0, full = slots[f, "up", h], tiles // 4

                    def pair(c, rep, cols, width):
                        for b, w in enumerate((wg, wu)):
                            for s in range(4):
                                load(c + 4 * b + s, rep, rows_of(w, 4 * s, 4, cols), 4, width)
                    with sp.Fori(0, full) as i:
                        pair(c0, 8 * i, bass.ds(i * NW + f0 * P, NW), NW)
                    if tiles % 4:
                        width = (tiles % 4) * P
                        pair(c0 + 8 * full, 0, bass.ds((f0 + 4 * full) * P, width), width)
                    cd = slots[f, "down", h]
                    for j in range(DB):
                        k = f0
                        for n in down_tiles(tiles):
                            load(cd, 0, rows_of(wd, k, n, slice(j * NW, (j + 1) * NW)), n, NW)
                            cd += 1
                            k += n

            def load_gains(i):
                name, n = GAIN_ROWS[i]
                src = a[name] if name == "hg_lb_logits" else a[name][0:1, 0:n * P]
                dst, r0 = (rows, col[name] - KD) if i else (mem_rows, 0)
                sp.dma_start(dst[r0:r0 + n, :], src.rearrange("l (r p) -> (l r) p", p=P)).then_inc(rows_in if i else mem_rows_in, 16)

            def load_mem(j):
                sp.dma_start(mem_nat[:, :, j * NW:(j + 1) * NW],
                             a["mem"][0].rearrange("(t p) n -> p t n", p=P)[:, :, j * NW:(j + 1) * NW]).then_inc(mem_in[j], 16)

            def load_memkv(c):
                b, s = divmod(c, 4)
                load(slots["memkv"] + c, 0, rows_of(a["xattn_w_kv"][0], 4 * s, 4, slice(b * NW, (b + 1) * NW)), 4, NW)

            sp.dma_start(ident[:], a["ident"]).then_inc(mem_rows_in, 16)
            load_mem(0)
            load_gains(0)
            load_memkv(0)
            for j in range(1, DB):
                load_mem(j)
                load_memkv(j)
            for i in range(1, len(GAIN_ROWS)):
                load_gains(i)
            for t in range(TT):
                sp.dma_start(x[:, t, :], a["x"][0, t * P:(t + 1) * P, :]).then_inc(x_in, 16)
            for c in range(DB, 8):
                load_memkv(c)
            sp.dma_start(mask_i[:], a["level_mask"]).then_inc(const_in, 16)
            sp.dma_start(causal[:], a["causal"]).then_inc(const_in, 16)
            sp.dma_start(freq[:], a["freq"]).then_inc(const_in, 16)
            with nc.allow_non_contiguous_dma(reason="one position for each partition"):
                for t in range(TT):
                    sp.dma_start(pos_i[:, t:t + 1], a["positions"][0, t * P:(t + 1) * P].rearrange("(p o) -> p o", o=1)).then_inc(const_in, 16)
            for n, name in enumerate(("mla_q_norm", "mla_k_norm")):
                sp.dma_start(pe_gain[:, n, :], a[name][0:1, P:QK].broadcast_to([P, ROPE])).then_inc(const_in, 16)
            load_ffn(1)
            for b, n in enumerate(MIX):
                for s in range(4):
                    load(M + 4 * b + s, 0, rows_of(a["w_in"][0], 4 * s, 4, slice(starts[n], starts[n] + MIX_WIDTH[n])), 4, MIX_WIDTH[n])
            for b in range(3):
                load(slots["q_up"] + b, 0, rows_of(a["mla_w_q_up"][0], 0, QR, slice(b * NW, (b + 1) * NW)), QR, NW)
            for b in range(2):
                load(slots["kv_up"] + b, 0, rows_of(a["mla_w_kv_up"][0], 0, KR, slice(2 * b * NW, 2 * (b + 1) * NW)), KR, 2 * NW)
            for n, k0 in (("w_out_hg", AH), ("w_out", 0)):
                for j in range(DB):
                    for s in range(2):
                        load(slots[n] + 2 * j + s, 0, rows_of(a["w_out"][0], k0 + 4 * s, 4, slice(j * NW, (j + 1) * NW)), 4, NW)
            for s in range(4):
                load(slots["xq"] + s, 0, rows_of(a["xattn_w_q"][0], 4 * s, 4, slice(0, NW)), 4, NW)
            for j in range(DB):
                load(slots["w_o"] + j, 0, rows_of(a["xattn_w_o"][0], 0, 4, slice(j * NW, (j + 1) * NW)), 4, NW)
            load_ffn(2)
            for j in range(DB):
                B = blocks[2, "down", 1] + j
                sp.wait_ge(acc_taken[B % 2], B // 2 + 1)
                sp.dma_start(out[0].rearrange("(t p) n -> p t n", p=P)[:, :, j * NW:(j + 1) * NW],
                             x[:, :, j * NW:(j + 1) * NW]).then_inc(out_done, 16)
            sp.wait_ge(out_done, 16 * DB)

        @block.gpsimd
        def _(pool):
            done = Done(pool, pool_done)

            def norm(name):
                n, width = NORMS[name]
                pool.wait_ge(ev("sums_" + name), 1)
                done(nc.gpsimd.tensor_scalar(cols(rsq, name), cols(sums, name), 1.0 / width, EPS, ALU.mult, ALU.add))
                done.wait()
                nc.gpsimd.tensor_tensor(cols(rsq, name), cols(rsq, name), half[:, 0:n], ALU.pow).then_inc(ev("rsq_" + name), 1)

            def complement(h):
                pool.wait_ge(ev("forget"), h + 1)
                if h:
                    pool.wait_ge(small_ready[1], STEPS)
                nc.gpsimd.tensor_scalar(kxT[:], bT[:], -1.0, 1.0, ALU.mult, ALU.add).then_inc(ev("complement"), 1)

            def differences(k):
                h, l = divmod(k, STEPS)
                if l == 0:
                    return
                if l == 1:
                    pool.wait_ge(ev("running"), h + 1)
                if k >= 2:
                    pool.wait_ge(small_ready[1], k - 1)
                m = 2 ** (l - 1)
                w = wave[:, k % 2, :].rearrange("p (n u m) -> p n u m", u=2, m=m)
                b = bT[:].rearrange("p h t -> p (h t)").rearrange("p (n u m) -> p n u m", u=2, m=m)
                mid = over(b[:, :, 0, m - 1], m)
                nc.gpsimd.tensor_tensor(w[:, :, 1, :], b[:, :, 1, :], mid, ALU.subtract)
                nc.gpsimd.tensor_tensor(w[:, :, 0, :], mid, b[:, :, 0, :], ALU.subtract).then_inc(ev("differences"), 1)

            done(nc.gpsimd.memset(half[:], -0.5))
            done.wait()
            norm("mem")
            norm("x1")
            kv = memkv[:].rearrange("p r (h c) -> p r h c", h=2)
            pool.wait_ge(ev("memkv"), 2)
            for b in range(2):
                for t in range(MT):
                    ins = nc.gpsimd.tensor_copy(memv[:, t, 2 * b * P:2 * (b + 1) * P].rearrange("p (h c) -> p h c", h=2),
                                                kv[:, b * MT + t, :, P:2 * P])
            ins.then_inc(ev("memv"), 1)
            norm("memk")
            norm("x2")
            complement(0)
            for k in range(STEPS):
                differences(k)
            norm("cq")
            norm("ckv")
            complement(1)
            for k in range(STEPS, 2 * STEPS):
                differences(k)
            def rotate_queries(t):
                g = nc.gpsimd
                for b in range(3):
                    pool.wait_ge(acc_taken[(blocks["q_up"] + b) % 2], (blocks["q_up"] + b) // 2 + 1)
                d4 = q_pe[:, t].rearrange("p h (u f) -> p h u f", u=2)
                c4, s4 = (q_tmp[:, i].rearrange("p h (u f) -> p h u f", u=2) for i in range(2))
                done(g.tensor_tensor(q_pe[:, t], q_nat[:, t, :].rearrange("p (h c) -> p h c", h=AH)[:, :, P:QK], under(pe_gain[:, 0, :], AH),
                                     ALU.mult))
                done.wait()
                for tmp, k in ((c4, 1), (s4, 0)):
                    done(g.tensor_tensor(tmp, d4, cs[:, k, t, :].unsqueeze(1).unsqueeze(1).broadcast_to([P, AH, 2, RH]), ALU.mult))
                done.wait()
                done(g.tensor_tensor(d4[:, :, 0, :], c4[:, :, 0, :], s4[:, :, 1, :], ALU.subtract))
                done(g.tensor_tensor(d4[:, :, 1, :], c4[:, :, 1, :], s4[:, :, 0, :], ALU.add))
                done.wait()

            rotate_queries(0)
            norm("hg")
            norm("q")
            rotate_queries(1)
            pool.sem_inc(ev("q_turned"), 1)
            norm("k")
            for name in ("o_mla", "x3", "xq", "x4"):
                norm(name)

        @block.scalar
        def _(act):
            done = Done(act, act_done)
            flat_stage = stage[:].rearrange("p a b -> p (a b)")

            def hi(c, rep, tiles, width):
                act.wait_ge(loaded[c % RAW], 16 * (c // RAW + 1) + rep * (16 // RAW))
                if c >= SPLIT:
                    act.wait_ge(slot_used, c + rep - SPLIT + 1)
                n = tiles * width
                nc.scalar.activation(w_hi[:, c % SPLIT, 0:n], raw[:, c % RAW, 0:n], ACT.Copy).then_inc(hi_done, 1)

            def turned_hi(dst, tile0, g, rep, gain=None, tiles=4, same=False):
                for b in range(2):
                    m0, n = b * -(-tiles // 2), (-(-tiles // 2), tiles // 2)[b]
                    act.wait_ge(tr_ready[b], g + rep + 1)
                    if gain is None or same:
                        ins = nc.scalar.activation(dst[:, bass.ds(tile0 + m0, n), :], tr[:, b, 0:n * SEQ].rearrange("p (k t) -> p k t", k=n),
                                                   ACT.Copy, scale=1.0 if gain is None else gains[:, gain:gain + 1])
                    else:
                        for m in range(n):
                            k = tile0 + m0 + m
                            ins = nc.scalar.activation(dst[:, k, :], tr[:, b, m * SEQ:(m + 1) * SEQ], ACT.Copy,
                                                       scale=gains[:, gain + k:gain + k + 1])
                    ins.then_inc(t_hi, 1)

            def turned(dst, tile0, g, gain=None):
                for b in range(2):
                    act.wait_ge(tr_ready[b], g + 1)
                    ins = nc.scalar.activation(dst[:, tile0 + 2 * b:tile0 + 2 * b + 2, :], tr[:, b, :].rearrange("p (k t) -> p k t", k=2),
                                               ACT.Copy, scale=1.0 if gain is None else gains[:, gain:gain + 1])
                    ins.then_inc(tr_taken[b], 1)

            def square_sums(name, src):
                for t in range(src.shape[1]):
                    done.wait()
                    ins = nc.scalar.activation(flat_stage[:, 0:src.shape[2]], src[:, t, :], ACT.Square, accum_out=cols(sums, name, t, 1))
                    if t == 0:
                        done(ins)
                ins.then_inc(ev("sums_" + name), 1)
                act.wait_ge(ev("sums_" + name), 1)

            def take(B, c_end, dst, func, scale, width=NW):
                act.wait_ge(slot_used, c_end)
                for t in range(TT):
                    ins = nc.scalar.activation(dst(t), acc[:, B % 2, t, 0:width], func, scale=scale[:, t:t + 1])
                ins.then_inc(acc_taken[B % 2], 1)

            def entry(name, s):
                key, gain = ENTRY[name]
                if s == 2:
                    turned_hi(hT_hi, 4 * (DB - 1), groups[key] + DB - 1, 0, gain=col[gain])
                if s == 3:
                    B = LAST_BLOCK[name]
                    act.wait_ge(acc_taken[B % 2], B // 2 + 1)
                    square_sums(name, x)

            def ffn(f, name):
                for h, (f0, tiles) in enumerate(HALVES):
                    c0, b0, g0 = slots[f, "up", h], blocks[f, "up", h], groups[f, "up", h]
                    full = tiles // 4

                    def pair(i, k, width=NW):
                        c, rep, prev = c0 + 8 * k, 8 * i, k > 0
                        for s in range(6):
                            if not (f == 2 and h == 0 and not prev and s == 0):
                                hi(c + s, rep, 4, width)
                            if prev and s == 3:
                                turned_hi(actT_hi, 4 * (i + k - 1), g0 + k - 1, i)
                            if not prev and h == 0 and f == 2:
                                entry(name, s)
                            if not prev and h == 0 and f == 1 and s == 1:
                                take_memkv(1)
                            if not prev and h == 0 and f == 1 and s == 5:
                                bound_and_angles()
                        if prev:
                            act.wait_ge(acc_taken[(b0 + 1) % 2], (b0 + 1) // 2 + k + i)
                        elif h == 0:
                            act.wait_ge(ev("rsq_" + name), 1)
                        act.wait_ge(slot_used, c + rep + 4)
                        for t in range(TT):
                            ins = nc.scalar.activation(gate[:, t, 0:width], acc[:, b0 % 2, t, 0:width], ACT.Silu, scale=cols(rsq, name, t, 1))
                        ins.then_inc(acc_taken[b0 % 2], 1)
                        if not prev and h == 0 and f == 1:
                            turned(memkT, 0, groups["memk"], gain=col["xattn_k_norm"])
                        hi(c + 6, rep, 4, width)
                        hi(c + 7, rep, 4, width)

                    pair(0, 0)
                    with act.Fori(0, full - 1) as i:
                        pair(i, 1)
                    last = full - 1
                    if tiles % 4:
                        last = full
                        pair(0, full, (tiles % 4) * P)
                    cd = slots[f, "down", h]
                    ns = down_tiles(tiles)
                    for j in range(DB):
                        for s in range(len(ns)):
                            hi(cd + len(ns) * j + s, 0, ns[s], NW)
                            if j == 0 and s == 3:
                                turned_hi(actT_hi, 4 * last, g0 + last, 0, tiles=tiles - 4 * last)
                            if j > 0 and s == 4 and h == 1 and f == 1:
                                turned_hi(hT_hi, 4 * (j - 1), groups[f, "down", h] + j - 1, 0, gain=col["mix_norm"])

            def bound_and_angles():
                act.wait_ge(ev("lb_shifted"), 1)
                nc.scalar.activation(lbt[:, 3:5, :], lbt[:, 1:3, :], ACT.Exp).then_inc(ev("lb_exp"), 1)
                act.wait_ge(ev("angles"), 1)
                nc.scalar.activation(cs[:].rearrange("p k t f -> p k (t f)"), rest[:], ACT.Sin).then_inc(ev("cos_sin"), 1)

            def take_memkv(b):
                if b == 0:
                    act.wait_ge(ev("rsq_mem"), 1)
                take(blocks["memkv"] + b, slots["memkv"] + 4 * b + 4, lambda t: memkv[:, b * MT + t, :], ACT.Copy, cols(rsq, "mem"))
                act.wait_ge(acc_taken[(blocks["memkv"] + b) % 2], (blocks["memkv"] + b) // 2 + 1)
                act.sem_inc(ev("memkv"), 1)

            def mem_turned(j):
                turned_hi(mT_hi, 4 * j, groups["mem"] + j, 0, gain=col["mem_norm"])

            def x_turned(j):
                turned_hi(hT_hi, 4 * j, groups["x"] + j, 0, gain=col["ffn1_norm"])

            act.wait_ge(ev("gains"), 1)
            for j in range(2):
                mem_turned(j)
                hi(j, 0, 4, NW)
            for j in range(2, DB):
                hi(j, 0, 4, NW)
                mem_turned(j)
            hi(4, 0, 4, NW)
            square_sums("mem", mem_nat)
            act.wait_ge(ev("gains"), 2)
            for j in range(3):
                hi(5 + j, 0, 4, NW)
                x_turned(j)
                if j == 0:
                    take_memkv(0)
                if j == 1:
                    square_sums("x1", x)
            x_turned(3)
            ffn(1, "x1")

            def mixer(m):
                if m < 4:
                    entry("x2", m)
                if m >= 5 and (m - 5) % 4 == 0 and (m - 5) // 4 < len(MIX):
                    b = (m - 5) // 4
                    n = MIX[b]
                    kind, h = n[:2], n[-1]
                    if b == 0:
                        act.wait_ge(ev("rsq_x2"), 1)
                    dst, func = {
                        "hf": (lambda t: gate[:, t, :], ACT.Sigmoid), "hq": (lambda t: nat[:, t, :], ACT.Copy),
                        "cq": (lambda t: gate[:, t, :], ACT.Copy), "ck": (lambda t: ckv_nat[:, t, :], ACT.Copy),
                        "hi": (lambda t: V[:, t, int(h) * NW:(int(h) + 1) * NW], ACT.Copy),
                        "hg": (lambda t: G[:, t, int(h) * NW:(int(h) + 1) * NW], ACT.Silu)}[kind]
                    take(blocks["mix"] + b, M + 4 * b + 4, dst, func, cols(rsq, "x2"), MIX_WIDTH[n])
                    if n in ("cq", "ckv"):
                        act.wait_ge(acc_taken[(blocks["mix"] + b) % 2], (blocks["mix"] + b) // 2 + 1)
                        src = gate if n == "cq" else ckv_nat[:, :, 0:KR * P]
                        if n == "ckv":
                            act.wait_ge(ev("sums_cq"), 1)
                        for t in range(TT):
                            ins = nc.scalar.activation(nat[:, t, 0:src.shape[2]], src[:, t, :], ACT.Square, accum_out=cols(sums, n, t, 1))
                        ins.then_inc(ev("sums_" + n), 1)
                for h, m0 in ((0, 6), (1, 26)):
                    if m == m0:
                        act.wait_ge(ev("forget"), h + 1)
                        nc.scalar.activation(lfT[:], bT[:], ACT.Ln).then_inc(ev("log_forget"), 1)
                    if m == m0 + 4:
                        turned(qxT, 0, groups[f"hq{h}"])
                if m == 14:
                    turned_hi(cqT_hi, 0, groups["cq"], 0, gain=col["mla_q_a_norm"])
                if m == 18:
                    turned_hi(ckvT_hi, 0, groups["ckv"], 0, gain=col["mla_kv_a_norm"], tiles=KR)
                for h in range(2):
                    l = m - STEP0[h]
                    if 1 <= l < STEPS:
                        k = h * STEPS + l
                        act.wait_ge(ev("differences"), h * (STEPS - 1) + l)
                        nc.scalar.activation(wave[:, k % 2, :], wave[:, k % 2, :], ACT.Exp).then_inc(ev("decays"), 1)
                for b in range(3):
                    if m == 42 + b:
                        if b == 0:
                            act.wait_ge(ev("rsq_cq"), 1)
                        take(blocks["q_up"] + b, slots["q_up"] + b + 1, lambda t: q_nat[:, t, b * NW:(b + 1) * NW], ACT.Copy, cols(rsq, "cq"))
                for h in range(2):
                    if m == 42 + 2 * h:
                        for t in range(TT):
                            act.wait_ge(small_ready[t], fills["av"] + h + 1)
                            nc.scalar.activation(stage[:, 2 * h + t, :], small[:, t, :], ACT.Square).then_inc(ev("hg_squares"), 1)

            def take_keys(b):
                if b == 0:
                    act.wait_ge(ev("rsq_ckv"), 1)
                take(blocks["kv_up"] + 2 * b, slots["kv_up"] + b + 1, lambda t: kv_nat[:, t, 2 * b * NW:(2 * b + 1) * NW],
                     ACT.Copy, cols(rsq, "ckv"))

            def head_squares(name, src, width, signal):
                for t in range(TT):
                    for h in range(AH):
                        if h % 4 == 0:
                            done.wait()
                        done(nc.scalar.activation(flat_stage[:, h % 4 * width:(h % 4 + 1) * width], src(t, h), ACT.Square,
                                                  accum_out=cols(sums, name, t * AH + h, 1)))
                done.wait()
                act.sem_inc(signal, 1)

            def query_squares():
                B = blocks["q_up"] + 2
                act.wait_ge(acc_taken[B % 2], B // 2 + 1)
                act.wait_ge(ev("first_half_summed"), 1)
                head_squares("q", lambda t, h: q_nat[:, t, h * QK:(h + 1) * QK], QK, ev("sums_q"))

            def key_squares():
                for B in (blocks["kv_up"] + 2, blocks["kv_up"] + 3):
                    act.wait_ge(acc_taken[B % 2], B // 2 + 1)
                head_squares("k", lambda t, h: kv_nat[:, t, h * 2 * P:h * 2 * P + P], P, ev("squares_k"))

            for m in range(40):
                hi(M + m, 0, 4, MIX_WIDTH[MIX[m // 4]])
                mixer(m)
            for m in range(40, 45):
                hi(M + m, 0, 4, NW)
                mixer(m)
            query_squares()
            take_keys(0)
            hi(slots["w_out_hg"], 0, 4, NW)
            take_keys(1)

            W, M_ = slots["w_out_hg"], slots["w_out"]
            for i in range(2):
                turned_hi(catT_hi, 8 + 4 * i, groups["cat_hg"] + i, 0, gain=col["hg_out_norm"], same=True)
            hi(W + 1, 0, 4, NW)
            key_squares()
            for i in range(2):
                turned(qTn, 4 * i, groups["qn"] + i, gain=col["mla_q_norm"])
            hi(W + 2, 0, 4, NW)
            act.wait_ge(ev("q_turned"), 1)
            for i in range(2):
                turned(kTn, 4 * i, groups["kn"] + i, gain=col["mla_k_norm"])
            hi(W + 3, 0, 4, NW)
            for b in range(2):
                act.wait_ge(tr_ready[b], groups["qp"] + 1)
                for n in range(2):
                    r = slice(n * ROPE, (n + 1) * ROPE)
                    ins = nc.scalar.activation(qTp[n][r, 2 * b:2 * b + 2, :], tr[r, b, :].rearrange("p (k t) -> p k t", k=2), ACT.Copy)
                ins.then_inc(tr_taken[b], 1)
            turned(kTp, 0, groups["kp"])
            hi(W + 4, 0, 4, NW)
            hi(W + 5, 0, 4, NW)

            def exps(p):
                act.wait_ge(ev("shifts"), p + 1)
                for b, keys in enumerate((SEQ, P)):
                    for n in range(2):
                        c, i = (p % 2) * 1024 + 2 * SEQ * b + n * keys, 2 * b + n
                        ins = nc.scalar.activation(flat_stage[:, c:c + keys], flat_stage[:, c:c + keys], ACT.Exp, scale=SCALE,
                                                   bias=smax[:, p, i:i + 1], accum_out=ssum[:, p, i:i + 1])
                ins.then_inc(ev("exps"), 1)

            def prob_turned(p):
                g = groups["prob"] + p
                for b in range(2):
                    n = (4, 2)[b] * P
                    act.wait_ge(tr_ready[b], g + 1)
                    nc.scalar.activation(probT[:, p % 2, 4 * P * b:4 * P * b + n], tr[:, b, 0:n], ACT.Copy).then_inc(tr_taken[b], 1)

            exps(0)
            hi(W + 6, 0, 4, NW)
            prob_turned(0)
            exps(1)
            exps(2)
            prob_turned(1)
            hi(W + 7, 0, 4, NW)
            prob_turned(2)
            exps(3)
            prob_turned(3)
            hi(M_, 0, 4, NW)
            act.wait_ge(ev("o_mla"), AH // 2)
            square_sums("o_mla", o_mla)
            for i in range(2):
                turned_hi(catT_hi, 4 * i, groups["cat_mla"] + i, 0, gain=col["mla_out_norm"])
            hi(M_ + 1, 0, 4, NW)

            for k in range(2, 2 * DB):
                hi(M_ + k, 0, 4, NW)
                if k >= 4 and k % 2 == 0:
                    turned_hi(hT_hi, 4 * (k // 2 - 2), groups["x_out"] + k // 2 - 2, 0, gain=col["xattn_norm"])

            for s in range(4):
                hi(slots["xq"] + s, 0, 4, NW)
                if s == 0:
                    turned_hi(hT_hi, 4 * (DB - 2), groups["x_out"] + DB - 2, 0, gain=col["xattn_norm"])
                entry("x3", s)
            hi(slots["w_o"], 0, 4, NW)
            act.wait_ge(ev("rsq_x3"), 1)
            act.wait_ge(slot_used, slots["xq"] + 4)
            for t in range(TT):
                for h in range(XH):
                    k = slice(h * P, (h + 1) * P)
                    ins = nc.scalar.activation(nat[:, t, k], acc[:, blocks["xq"] % 2, t, k], ACT.Square, scale=cols(rsq, "x3", t, 1),
                                               accum_out=cols(sums, "xq", t * XH + h, 1))
                ins.then_inc(ev("xq_squared"), 1)
            act.wait_ge(ev("xq_squared"), TT)
            act.sem_inc(ev("sums_xq"), 1)
            hi(slots["w_o"] + 1, 0, 4, NW)
            turned(xqT, 0, groups["xq"], gain=col["xattn_q_norm"])
            for p in range(XH // 2):
                for t in range(TT):
                    act.wait_ge(ev("x_shifts"), TT * p + t + 1)
                    for n in range(2):
                        k = slice(n * MEM, (n + 1) * MEM)
                        ins = nc.scalar.activation(stage[:, 2 * p + t, k], small[:, t, k], ACT.Exp, scale=X_SCALE,
                                                   bias=smax[:, p, 2 * t + n:2 * t + n + 1], accum_out=ssum[:, p, 2 * t + n:2 * t + n + 1])
                    ins.then_inc(small_taken[t], 1)
                for t in range(TT):
                    act.wait_ge(small_taken[t], fills["xattn"] + p + 1)
                act.sem_inc(ev("x_exps"), 1)
            for p in range(XH // 2):
                for t in range(TT):
                    act.wait_ge(tr_ready[t], groups["x_prob"] + p + 1)
                    nc.scalar.activation(x_probT[:, p, t, :], tr[:, t, :], ACT.Copy).then_inc(tr_taken[t], 1)
            turned_hi(xoT_hi, 0, groups["xo"], 0)
            for j in range(2, DB):
                hi(slots["w_o"] + j, 0, 4, NW)
            turned_hi(hT_hi, 0, groups["x_o"], 0, gain=col["ffn2_norm"])
            hi(slots[2, "up", 0], 0, 4, NW)
            for j in range(1, DB - 1):
                turned_hi(hT_hi, 4 * j, groups["x_o"] + j, 0, gain=col["ffn2_norm"])
            ffn(2, "x4")

        @block.vector
        def _(dve):
            done = Done(dve, dve_done)
            v = nc.vector
            flat_stage = stage[:].rearrange("p a b -> p (a b)")

            def lo(c, rep, tiles, width):
                dve.wait_ge(hi_done, c + rep + 1)
                n = tiles * width
                v.tensor_tensor(w_lo[:, c % SPLIT, 0:n], raw[:, c % RAW, 0:n],
                                w_hi[:, c % SPLIT, 0:n].bitcast(F32), ALU.subtract).then_inc(lo_done, 1)

            def turned_lo(dst_hi, dst, tile0, g, rep, h, hrep, gain=None, tiles=4, same=False):
                for b in range(2):
                    m0, n = b * -(-tiles // 2), (-(-tiles // 2), tiles // 2)[b]
                    dve.wait_ge(t_hi, 2 * h + b + 1 + 2 * hrep)
                    at_, src = bass.ds(tile0 + m0, n), tr[:, b, 0:n * SEQ].rearrange("p (k t) -> p k t", k=n)
                    if gain is None:
                        ins = v.tensor_tensor(dst[:, at_, :], src, dst_hi[:, at_, :].bitcast(F32), ALU.subtract)
                    elif same:
                        ins = v.scalar_tensor_tensor(dst[:, at_, :], src, gains[:, gain:gain + 1], dst_hi[:, at_, :].bitcast(F32),
                                                     ALU.mult, ALU.subtract)
                    else:
                        for m in range(n):
                            k = tile0 + m0 + m
                            ins = v.scalar_tensor_tensor(dst[:, k, :], src[:, m, :], gains[:, gain + k:gain + k + 1],
                                                         dst_hi[:, k, :].bitcast(F32), ALU.mult, ALU.subtract)
                    ins.then_inc(tr_taken[b], 1)

            def add_block(B, c_end, j, factor):
                dve.wait_ge(slot_used, c_end)
                for t in range(TT):
                    ins = v.scalar_tensor_tensor(x[:, t, j * NW:(j + 1) * NW], acc[:, B % 2, t, :], factor,
                                                 x[:, t, j * NW:(j + 1) * NW], ALU.mult, ALU.add)
                ins.then_inc(acc_taken[B % 2], 1)

            def entry(name, s, c):
                key, gain = ENTRY[name]
                if s == 1:
                    add_block(LAST_BLOCK[name], c, DB - 1, FACTOR[name])
                if s == 2:
                    turned_lo(hT_hi, hT_lo, 4 * (DB - 1), groups[key] + DB - 1, 0, splits[key] + DB - 1, 0, gain=col[gain])

            def ffn(f, name):
                for h, (f0, tiles) in enumerate(HALVES):
                    c0, b0, g0, h0 = slots[f, "up", h], blocks[f, "up", h], groups[f, "up", h], splits[f, "up", h]
                    full = tiles // 4

                    def up(i, k, width):
                        B = b0 + 1
                        dve.wait_ge(slot_used, c0 + 8 * k + 8 + 8 * i)
                        dve.wait_ge(acc_taken[b0 % 2], b0 // 2 + k + 1 + i)
                        for t in range(TT):
                            ins = v.scalar_tensor_tensor(nat[:, t, 0:width], acc[:, B % 2, t, 0:width], cols(rsq, name, t, 1),
                                                         gate[:, t, 0:width], ALU.mult, ALU.mult)
                        ins.then_inc(acc_taken[B % 2], 1)

                    def pair(i, k, width=NW):
                        c, rep, prev = c0 + 8 * k, 8 * i, k > 0
                        for s in range(8):
                            if not (f == 2 and h == 0 and not prev and s == 0):
                                lo(c + s, rep, 4, width)
                            if prev and s == 1:
                                up(i, k - 1, NW)
                            if prev and s == 3:
                                turned_lo(actT_hi, actT_lo, 4 * (i + k - 1), g0 + k - 1, i, h0 + k - 1, i)
                            if not prev and h == 1 and s == 1:
                                add_block(b0 - 1, c0, DB - 1, 0.5)
                            if not prev and h == 0 and f == 2:
                                entry(name, s, c0)
                            if not prev and h == 0 and f == 1:
                                memory_keys(s)
                                if s == 4:
                                    angles()
                                if s == 7:
                                    lower_bound()

                    pair(0, 0)
                    with dve.Fori(0, full - 1) as i:
                        pair(i, 1)
                    width, last = NW, full - 1
                    if tiles % 4:
                        width, last = (tiles % 4) * P, full
                        pair(0, full, width)
                    cd, bd = slots[f, "down", h], blocks[f, "down", h]
                    ns = down_tiles(tiles)
                    for j in range(DB):
                        for s in range(len(ns)):
                            lo(cd + len(ns) * j + s, 0, ns[s], NW)
                            if j == 0 and s == 1:
                                up(0, last, width)
                            if j == 0 and s == 3:
                                turned_lo(actT_hi, actT_lo, 4 * last, g0 + last, 0, h0 + last, 0, tiles=tiles - 4 * last)
                            if j > 0 and s == 1:
                                add_block(bd + j - 1, cd + len(ns) * j, j - 1, 0.5)
                            if j > 0 and s == 4 and h == 1 and f == 1:
                                turned_lo(hT_hi, hT_lo, 4 * (j - 1), groups[f, "down", h] + j - 1, 0, splits[f, "down", h] + j - 1, 0,
                                          gain=col["mix_norm"])

            def memory_keys(s):
                k = memkv[:].rearrange("p r (h c) -> p (r h) c", h=2)[:, :, 0:P]
                if s == 2:
                    dve.wait_ge(ev("memkv"), 2)
                    done(v.tensor_tensor(memk[:], k, k, ALU.mult))
                    done.wait()
                    v.tensor_reduce(cols(sums, "memk"), memk[:], AX, ALU.add).then_inc(ev("sums_memk"), 1)
                if s == 3:
                    dve.wait_ge(ev("rsq_memk"), 1)
                    dve.wait_ge(ev("sums_memk"), 1)
                    v.tensor_tensor(memk[:], k, over(cols(rsq, "memk"), P), ALU.mult).then_inc(ev("memk"), 1)

            def angles():
                L = gains[:, col["hg_lb_logits"]:col["hg_lb_logits"] + 2 * HG].rearrange("p (l h) -> p l h", l=2)
                done(v.tensor_tensor(lbt[:, 0, :], L[:, 0, :], L[:, 1, :], ALU.max))
                done.wait()
                v.tensor_tensor(lbt[:, 1:3, :], L, under(lbt[:, 0, :], 2), ALU.subtract).then_inc(ev("lb_shifted"), 1)
                dve.wait_ge(const_in, 16 * (3 + TT + 2))
                done(v.tensor_copy(level_mask[:], mask_i[:]))
                done(v.tensor_copy(pos_f[:], pos_i[:]))
                done.wait()
                for k in range(2):
                    for t in range(TT):
                        done(v.tensor_scalar(ang[:, k, t * RH:(t + 1) * RH], freq[:], pos_f[:, t:t + 1], None, ALU.mult))
                done.wait()
                for k in range(2):
                    done(v.tensor_scalar(turns[:, k, :], ang[:, k, :], 1.0 / TWO_PI, 0.25 * k, ALU.mult, ALU.add))
                for shift in (ROUND, -ROUND):
                    done.wait()
                    done(v.tensor_scalar(turns[:], turns[:], shift, None, ALU.add))
                done.wait()
                for n, part in enumerate((PI_1, PI_2, PI_3)):
                    done(v.scalar_tensor_tensor(rest[:], turns[:], -part, ang[:] if n == 0 else rest[:], ALU.mult, ALU.add))
                    done.wait()
                done(v.tensor_scalar(rest[:, 1, :], rest[:, 1, :], TWO_PI / 4, None, ALU.add))
                done.wait()
                v.tensor_scalar(rest[:], rest[:], 3.1415925, -3.1415925, ALU.min, ALU.max).then_inc(ev("angles"), 1)

            def lower_bound():
                dve.wait_ge(ev("lb_exp"), 1)
                done(v.tensor_tensor(lbt[:, 5, :], lbt[:, 3, :], lbt[:, 4, :], ALU.add))
                done.wait()
                done(v.reciprocal(lbt[:, 0, :], lbt[:, 5, :]))
                done.wait()
                done(v.tensor_tensor(bound[:, 0, :], lbt[:, 3, :], lbt[:, 0, :], ALU.mult))
                done.wait()
                done(v.tensor_scalar(bound[:, 1, :], bound[:, 0, :], -1.0, 1.0, ALU.mult, ALU.add))

            dve.wait_ge(ev("gains_turned"), 1)
            v.tensor_copy(gains[:, 0:KD], small[:, 0, 0:KD]).then_inc(ev("gains"), 1)
            dve.wait_ge(ev("gains"), 1)

            def mem_lo(j):
                turned_lo(mT_hi, mT_lo, 4 * j, groups["mem"] + j, 0, splits["mem"] + j, 0, gain=col["mem_norm"])

            def x_lo(j):
                turned_lo(hT_hi, hT_lo, 4 * j, groups["x"] + j, 0, splits["x"] + j, 0, gain=col["ffn1_norm"])

            for j in range(2):
                mem_lo(j)
                lo(j, 0, 4, NW)
            for j in range(2, DB):
                lo(j, 0, 4, NW)
                mem_lo(j)
            lo(4, 0, 4, NW)
            dve.wait_ge(ev("gains_turned"), 2)
            v.tensor_copy(gains[:, KD:N_ROWS], small[:, 1, 0:N_ROWS - KD]).then_inc(ev("gains"), 1)
            dve.wait_ge(ev("gains"), 2)
            for j in range(3):
                lo(5 + j, 0, 4, NW)
                x_lo(j)
            x_lo(3)
            ffn(1, "x1")

            def step_products(k):
                h, l = divmod(k, STEPS)
                if l == 0:
                    return
                m = 2 ** (l - 1)
                w = wave[:, k % 2, :].rearrange("p (n u m) -> p n u m", u=2, m=m)
                dve.wait_ge(ev("decays"), h * (STEPS - 1) + l)
                for u, src in ((1, qxT), (0, kxT)):
                    s = src[:].rearrange("p h t -> p (h t)").rearrange("p (n u m) -> p n u m", u=2, m=m)
                    ins = v.tensor_tensor(w[:, :, u, :], w[:, :, u, :], s[:, :, u, :], ALU.mult)
                ins.then_inc(ev("waves"), 1)

            def step_take(k):
                h, l = divmod(k, STEPS)
                for b in range(2):
                    dve.wait_ge(small_ready[b], fills["steps"] + k + 1)
                    src = small[:, b, :].rearrange("p (h t) -> p h t", h=HH)
                    if l == 0:
                        ins = v.tensor_tensor(AT[:, h * HH:(h + 1) * HH, b, :], src, under(ident[:], HH), ALU.mult)
                    elif l < LEVELS:
                        if b == 0:
                            dve.wait_ge(small_taken[1], k)
                        m = 2 ** (l - 1)
                        mask = uppers(level_mask[:, l, :], l).unsqueeze(1).broadcast_to([P, HH, HALF // m, m])
                        ins = v.copy_predicated(AT[:, h * HH:(h + 1) * HH, b, :].rearrange("p h (n u m) -> p h n u m", u=2, m=m)[:, :, :, 1, :], mask,
                                                small[:, b, 0:HH * HALF].rearrange("p (h n m) -> p h n m", h=HH, m=m))
                    else:
                        ins = v.tensor_copy(AT[:, h * HH + 2 * b:h * HH + 2 * b + 2, 2, :], src[:, 0:2, :])
                    ins.then_inc(small_taken[b], 1)

            def mixer(m):
                if m < 4:
                    entry("x2", m, M)
                for h, m0 in ((0, 6), (1, 26)):
                    if m == m0:
                        for b in range(2):
                            dve.wait_ge(tr_ready[b], groups[f"hf{h}"] + 1)
                            for i in range(2):
                                n = 2 * b + i
                                c = h * HH + n
                                ins = v.tensor_scalar(bT[:, n, :], tr[:, b, i * SEQ:(i + 1) * SEQ], bound[:, 1, c:c + 1], bound[:, 0, c:c + 1],
                                                      ALU.mult, ALU.add)
                            ins.then_inc(tr_taken[b], 1)
                        for b in range(2):
                            dve.wait_ge(tr_taken[b], groups[f"hf{h}"] + 1)
                        dve.sem_inc(ev("forget"), 1)
                    if m == m0 + 1:
                        dve.wait_ge(ev("log_forget"), h + 1)
                        dve.wait_ge(ev("complement"), h + 1)
                        for n in range(HH):
                            ins = v.tensor_tensor_scan(bT[:, n, :], one[:, 0:1].broadcast_to([P, SEQ]), lfT[:, n, :], 0.0, ALU.mult, ALU.add)
                        ins.then_inc(ev("running"), 1)
                if m == 14:
                    turned_lo(cqT_hi, cqT_lo, 0, groups["cq"], 0, splits["cq"], 0, gain=col["mla_q_a_norm"])
                if m == 18:
                    turned_lo(ckvT_hi, ckvT_lo, 0, groups["ckv"], 0, splits["ckv"], 0, gain=col["mla_kv_a_norm"], tiles=KR)
                for h in range(2):
                    if 0 <= m - 2 - STEP0[h] < STEPS:
                        step_take(h * STEPS + m - 2 - STEP0[h])
                    if 0 <= m - STEP0[h] < STEPS:
                        step_products(h * STEPS + m - STEP0[h])
                if m == 24:
                    rotary_keys()
                for h in range(2):
                    if m == 42 + 2 * h:
                        recurrence_outputs(h)

            def take_keys(b):
                B = blocks["kv_up"] + 2 * b + 1
                dve.wait_ge(ev("rsq_ckv"), 1)
                dve.wait_ge(slot_used, slots["kv_up"] + b + 1)
                for t in range(TT):
                    ins = v.tensor_scalar(kv_nat[:, t, (2 * b + 1) * NW:(2 * b + 2) * NW], acc[:, B % 2, t, :], cols(rsq, "ckv", t, 1), None, ALU.mult)
                ins.then_inc(acc_taken[B % 2], 1)

            kpe = ckv_nat[:, :, KR * P:KR * P + ROPE]

            def rotary_keys():
                B = blocks["mix"] + MIX.index("ckv")
                dve.wait_ge(acc_taken[B % 2], B // 2 + 1)
                dve.wait_ge(ev("cos_sin"), 1)
                done(v.tensor_tensor(k_sq[:], kpe, kpe, ALU.mult))
                done.wait()
                done(v.tensor_reduce(sums[:, KPE:KPE + TT], k_sq[:], AX, ALU.add))
                done(v.tensor_tensor(kpe, kpe, under(pe_gain[:, 1, :], TT), ALU.mult))
                done.wait()
                for t in range(TT):
                    d4 = kpe[:, t, :].rearrange("p (u f) -> p u f", u=2)
                    c4, s4 = (k_tmp[:, i].rearrange("p (u f) -> p u f", u=2) for i in range(2))
                    for tmp, k in ((c4, 1), (s4, 0)):
                        done(v.tensor_tensor(tmp, d4, under(cs[:, k, t, :], 2), ALU.mult))
                    done.wait()
                    done(v.tensor_tensor(d4[:, 0, :], c4[:, 0, :], s4[:, 1, :], ALU.subtract))
                    done(v.tensor_tensor(d4[:, 1, :], c4[:, 1, :], s4[:, 0, :], ALU.add))
                    done.wait()

            def recurrence_outputs(h):
                for t in range(TT):
                    cols_h = slice(h * NW, (h + 1) * NW)
                    dve.wait_ge(ev("hg_squares"), 2 * h + t + 1)
                    if h == 0 and t == 0:
                        B = blocks["mix"] + MIX.index("hg1")
                        dve.wait_ge(acc_taken[B % 2], B // 2 + 1)
                    v.tensor_tensor(o_hg[:, t, cols_h], small[:, t, :], G[:, t, cols_h], ALU.mult).then_inc(small_taken[t], 1)
                    done(v.tensor_reduce(cols(sums, "hg", t * HG + h * HH, HH), stage[:, 2 * h + t, :].rearrange("p (h c) -> p h c", h=HH), AX, ALU.add))
                done.wait()
                dve.sem_inc(ev(("first_half_summed", "sums_hg")[h]), 1)

            done(v.memset(one[:], 1.0))
            done.wait()
            for m in range(40):
                lo(M + m, 0, 4, MIX_WIDTH[MIX[m // 4]])
                mixer(m)
            for m in range(40, 45):
                lo(M + m, 0, 4, NW)
                mixer(m)
            take_keys(0)
            lo(slots["w_out_hg"], 0, 4, NW)
            dve.wait_ge(ev("rsq_hg"), 1)
            for t in range(TT):
                o = o_hg[:, t, :].rearrange("p (h c) -> p h c", h=HG)
                done(v.tensor_tensor(o, o, over(cols(rsq, "hg", t * HG, HG), P), ALU.mult))
            done.wait()
            dve.sem_inc(ev("hg_scaled"), 1)
            take_keys(1)

            W, M_ = slots["w_out_hg"], slots["w_out"]

            def add_recurrence(j):
                add_block(blocks["w_out_hg"] + j, W + 2 * j + 2, j, 1.0)

            for i in range(2):
                turned_lo(catT_hi, catT_lo, 8 + 4 * i, groups["cat_hg"] + i, 0, splits["cat_hg"] + i, 0, gain=col["hg_out_norm"], same=True)
            dve.wait_ge(ev("rsq_q"), 1)
            for t in range(TT):
                q = q_nat[:, t, :].rearrange("p (h c) -> p h c", h=AH)[:, :, 0:P]
                done(v.tensor_tensor(q, q, over(cols(rsq, "q", t * AH, AH), P), ALU.mult))
            done.wait()
            dve.sem_inc(ev("q_scaled"), 1)
            lo(W + 1, 0, 4, NW)
            dve.wait_ge(ev("squares_k"), 1)
            for t in range(TT):
                done(v.tensor_scalar(cols(sums, "k", t * AH, AH), cols(sums, "k", t * AH, AH), sums[:, KPE + t:KPE + t + 1], None, ALU.add))
            done.wait()
            dve.sem_inc(ev("sums_k"), 1)
            dve.wait_ge(ev("rsq_k"), 1)
            for t in range(TT):
                k = kv_nat[:, t, :].rearrange("p (h c) -> p h c", h=AH)[:, :, 0:P]
                done(v.tensor_tensor(k, k, over(cols(rsq, "k", t * AH, AH), P), ALU.mult))
            done.wait()
            dve.sem_inc(ev("k_scaled"), 1)
            lo(W + 2, 0, 4, NW)
            for t in range(TT):
                done(v.tensor_tensor(k_pe[:, t], under(kpe[:, t, :], AH), over(cols(rsq, "k", t * AH, AH), ROPE), ALU.mult))
            done.wait()
            dve.sem_inc(ev("k_rotated"), 1)
            dve.wait_ge(ev("q_turned"), 1)
            for t in range(TT):
                done(v.tensor_tensor(q_pe[:, t], q_pe[:, t], over(cols(rsq, "q", t * AH, AH), ROPE), ALU.mult))
            dve.wait_ge(tr_ready[1], groups["qn"] + 2)
            for n in range(2):
                done(v.memset(qTp[n][(1 - n) * ROPE:(2 - n) * ROPE], 0.0))
            done.wait()
            dve.sem_inc(ev("q_rotated"), 1)
            lo(W + 3, 0, 4, NW)
            add_recurrence(0)
            lo(W + 4, 0, 4, NW)
            lo(W + 5, 0, 4, NW)
            add_recurrence(1)

            KEYS = (SEQ, P)

            def parts(p):
                base_ = (p % 2) * 1024
                return [flat_stage[:, base_ + 2 * SEQ * b:base_ + 2 * SEQ * b + 2 * KEYS[b]].rearrange("p (h k) -> p h k", h=2) for b in range(2)]

            score_fill, out_fill = FILL_ORDER
            def shift(p):
                if p >= 2:
                    dve.wait_ge(tr_ready[1], groups["prob"] + p - 1)
                for b, s in enumerate(parts(p)):
                    dve.wait_ge(small_ready[b], fills["mla"] + score_fill[p] + 1)
                    v.tensor_tensor(s, small[:, b, 0:2 * KEYS[b]].rearrange("p (h k) -> p h k", h=2), under(causal[:, SEQ - KEYS[b]:SEQ], 2),
                                    ALU.add).then_inc(small_taken[b], 1)
                for b, s in enumerate(parts(p)):
                    dve.wait_ge(small_taken[b], fills["mla"] + score_fill[p] + 1)
                    done(v.tensor_reduce(smax[:, p, 2 * b:2 * b + 2], s, AX, ALU.max))
                done.wait()
                v.tensor_scalar(smax[:, p, :], smax[:, p, :], -SCALE, None, ALU.mult).then_inc(ev("shifts"), 1)

            def outputs(p):
                dve.wait_ge(ev("exps"), p + 1)
                done(v.reciprocal(srec[:, p, :], ssum[:, p, :]))
                done.wait()
                for b in range(2):
                    dve.wait_ge(small_ready[b], fills["mla"] + out_fill[p] + 1)
                    v.tensor_tensor(o_mla[:, 1 - b, 2 * p * P:2 * (p + 1) * P].rearrange("p (h c) -> p h c", h=2),
                                    small[:, b, 0:2 * P].rearrange("p (h c) -> p h c", h=2), over(srec[:, p, 2 * b:2 * b + 2], P),
                                    ALU.mult).then_inc(small_taken[b], 1)
                for b in range(2):
                    dve.wait_ge(small_taken[b], fills["mla"] + out_fill[p] + 1)
                dve.sem_inc(ev("o_mla"), 1)

            shift(0)
            shift(1)
            lo(W + 6, 0, 4, NW)
            shift(2)
            outputs(0)
            add_recurrence(2)
            shift(3)
            lo(W + 7, 0, 4, NW)
            outputs(1)
            outputs(2)
            outputs(3)
            lo(M_, 0, 4, NW)
            dve.wait_ge(ev("rsq_o_mla"), 1)
            for t in range(TT):
                done(v.tensor_scalar(o_mla[:, t, :], o_mla[:, t, :], cols(rsq, "o_mla", t, 1), None, ALU.mult))
            done.wait()
            dve.sem_inc(ev("o_scaled"), 1)
            for i in range(2):
                turned_lo(catT_hi, catT_lo, 4 * i, groups["cat_mla"] + i, 0, splits["cat_mla"] + i, 0, gain=col["mla_out_norm"])
            add_recurrence(3)
            lo(M_ + 1, 0, 4, NW)

            for k in range(2, 2 * DB):
                lo(M_ + k, 0, 4, NW)
                if k % 2:
                    add_block(blocks["w_out"] + k // 2 - 1, M_ + k - 1, k // 2 - 1, 1.0)
                elif k >= 4:
                    turned_lo(hT_hi, hT_lo, 4 * (k // 2 - 2), groups["x_out"] + k // 2 - 2, 0, splits["x_out"] + k // 2 - 2, 0, gain=col["xattn_norm"])

            for s in range(4):
                lo(slots["xq"] + s, 0, 4, NW)
                if s == 0:
                    turned_lo(hT_hi, hT_lo, 4 * (DB - 2), groups["x_out"] + DB - 2, 0, splits["x_out"] + DB - 2, 0, gain=col["xattn_norm"])
                entry("x3", s, slots["xq"])
            lo(slots["w_o"], 0, 4, NW)
            dve.wait_ge(ev("rsq_x3"), 1)
            for t in range(TT):
                dve.wait_ge(ev("xq_squared"), t + 1)
                ins = v.tensor_scalar(gate[:, t, :], acc[:, blocks["xq"] % 2, t, :], cols(rsq, "x3", t, 1), None, ALU.mult)
            ins.then_inc(acc_taken[blocks["xq"] % 2], 1)
            dve.wait_ge(acc_taken[blocks["xq"] % 2], blocks["xq"] // 2 + 1)
            dve.wait_ge(ev("rsq_xq"), 1)
            q = gate.rearrange("p t (h c) -> p (t h) c", h=XH)
            v.tensor_tensor(q, q, over(cols(rsq, "xq"), P), ALU.mult).then_inc(ev("xq_scaled"), 1)
            lo(slots["w_o"] + 1, 0, 4, NW)
            for p in range(XH // 2):
                for t in range(TT):
                    dve.wait_ge(small_ready[t], fills["xattn"] + p + 1)
                    done(v.tensor_reduce(smax[:, p, 2 * t:2 * t + 2], small[:, t, :].rearrange("p (h k) -> p h k", h=2), AX, ALU.max))
                    done.wait()
                    v.tensor_scalar(smax[:, p, 2 * t:2 * t + 2], smax[:, p, 2 * t:2 * t + 2], -X_SCALE, None, ALU.mult).then_inc(ev("x_shifts"), 1)
            for p in range(XH // 2):
                dve.wait_ge(ev("x_exps"), p + 1)
                done(v.reciprocal(srec[:, p, :], ssum[:, p, :]))
            done.wait()
            for p in range(XH // 2):
                for t in range(TT):
                    dve.wait_ge(small_ready[t], fills["xattn"] + XH // 2 + p + 1)
                    v.tensor_tensor(xo[:, t, 2 * p * P:2 * (p + 1) * P].rearrange("p (h c) -> p h c", h=2),
                                    small[:, t, 0:2 * P].rearrange("p (h c) -> p h c", h=2), over(srec[:, p, 2 * t:2 * t + 2], P),
                                    ALU.mult).then_inc(small_taken[t], 1)
            turned_lo(xoT_hi, xoT_lo, 0, groups["xo"], 0, splits["xo"], 0)
            for j in range(2, DB):
                lo(slots["w_o"] + j, 0, 4, NW)
                add_block(blocks["w_o"] + j - 2, slots["w_o"] + j - 1, j - 2, 1.0)
            turned_lo(hT_hi, hT_lo, 0, groups["x_o"], 0, splits["x_o"], 0, gain=col["ffn2_norm"])
            lo(slots[2, "up", 0], 0, 4, NW)
            add_block(blocks["w_o"] + DB - 2, slots["w_o"] + DB - 1, DB - 2, 1.0)
            for j in range(1, DB - 1):
                turned_lo(hT_hi, hT_lo, 4 * j, groups["x_o"] + j, 0, splits["x_o"] + j, 0, gain=col["ffn2_norm"])
            ffn(2, "x4")
            add_block(blocks[2, "down", 1] + DB - 1, slots[2, "down", 1] + len(down_tiles(HALVES[1][1])) * DB, DB - 1, 0.5)

        @block.tensor
        def _(pe):
            mm = nc.tensor.matmul

            def turn(g, rep, srcs):
                for b in range(2):
                    if g:
                        pe.wait_ge(tr_taken[b], g + rep)
                    for n, s in enumerate(srcs[b]):
                        ins = nc.tensor.transpose(tr[:, b, n * P:(n + 1) * P], s, ident[:])
                    ins.then_inc(tr_ready[b], 1)

            def turn_features(g, rep, part, tiles=4):
                h = -(-tiles // 2)
                turn(g, rep, [[part(m, t) for m in ms for t in range(TT)] for ms in (range(h), range(h, tiles))])

            def of(src, col0=0):
                return lambda m, t: src[:, t, col0 + m * P:col0 + (m + 1) * P]

            def slot(c, rep, B, lhs_hi, lhs_lo, k0, tiles, width, first, last, off=0, full=None, signal=True):
                pe.wait_ge(lo_done, c + rep + 1)
                full = full or width
                for kk in range(tiles):
                    w0 = kk * full + off
                    wh, wl = w_hi[:, c % SPLIT, w0:w0 + width], w_lo[:, c % SPLIT, w0:w0 + width]
                    for t in range(TT):
                        dst = acc[:, B % 2, t, 0:width]
                        xh = lhs_hi[:, k0 + kk, t * P:(t + 1) * P]
                        xl = lhs_lo[:, k0 + kk, t * P:(t + 1) * P]
                        mm(dst, xh, wh, start=first and kk == 0, stop=False)
                        mm(dst, xl, wh, start=False, stop=False)
                        ins = mm(dst, xh, wl, start=False, stop=last and kk == tiles - 1)
                if signal:
                    ins.then_inc(slot_used, 1)

            def free(B, k=0, i=0):
                if B + 2 * k >= 2:
                    pe.wait_ge(acc_taken[B % 2], B // 2 + k + i)

            def stands(B):
                pe.wait_ge(acc_taken[B % 2], B // 2 + 1)

            def split_stands(g):
                for b in range(2):
                    pe.wait_ge(tr_taken[b], g + 1)

            def entry(name, s):
                g = groups[ENTRY[name][0]] + DB - 1
                if s == 1:
                    stands(LAST_BLOCK[name])
                    turn_features(g, 0, of(x, (DB - 1) * NW))
                if s == 2:
                    split_stands(g)

            def fill(f, b):
                if f:
                    pe.wait_ge(small_taken[b], f)

            def ffn(f, name):
                for h, (f0, tiles) in enumerate(HALVES):
                    c0, b0, g0 = slots[f, "up", h], blocks[f, "up", h], groups[f, "up", h]
                    full = tiles // 4

                    def pair(i, k, width=NW):
                        c, rep, prev = c0 + 8 * k, 8 * i, k > 0
                        for b in range(2):
                            B = b0 + b
                            free(B, k, i)
                            for s in range(4):
                                slot(c + 4 * b + s, rep, B, hT_hi, hT_lo, 4 * s, 4, width, s == 0, s == 3)
                                if prev and b == 0 and s == 1:
                                    pe.wait_ge(acc_taken[(b0 + 1) % 2], (b0 + 1) // 2 + k + i)
                                    turn_features(g0 + k - 1, i, of(nat))
                                if not prev and b == 0 and h == 0 and f == 2:
                                    entry(name, s)
                                if not prev and b == 1 and h == 0 and f == 1 and s == 0:
                                    pe.wait_ge(ev("memk"), 1)
                                    turn_features(groups["memk"], 0, lambda m, t: memk[:, ((m // 2) * MT + t) * 2 + m % 2, :])

                    pair(0, 0)
                    with pe.Fori(0, full - 1) as i:
                        pair(i, 1)
                    last = full - 1
                    if tiles % 4:
                        last = full
                        pair(0, full, (tiles % 4) * P)
                    cd, bd = slots[f, "down", h], blocks[f, "down", h]
                    ns = down_tiles(tiles)
                    for j in range(DB):
                        B = bd + j
                        free(B)
                        k = 0
                        for s in range(len(ns)):
                            if j == 0 and s == last:
                                split_stands(g0 + last)
                            slot(cd + len(ns) * j + s, 0, B, actT_hi, actT_lo, k, ns[s], NW, s == 0, s == len(ns) - 1)
                            k += ns[s]
                            if j == 0 and s == 1:
                                pe.wait_ge(acc_taken[(b0 + 1) % 2], (b0 + 1) // 2 + last + 1)
                                turn_features(g0 + last, 0, of(nat), tiles - 4 * last)
                            if j > 0 and s == 2 and h == 1 and f == 1:
                                stands(B - 1)
                                turn_features(groups[f, "down", h] + j - 1, 0, of(x, (j - 1) * NW))

            def turn_mem(j):
                pe.wait_ge(mem_in[j], 16)
                turn_features(groups["mem"] + j, 0, of(mem_nat, j * NW))

            pe.wait_ge(mem_rows_in, 16 * 2)
            nc.tensor.transpose(small[:, 0, 0:KD], mem_rows[0:KD, :], ident[0:KD, 0:KD]).then_inc(ev("gains_turned"), 1)
            turn_mem(0)
            turn_mem(1)
            for b in range(2):
                for s in range(4):
                    if b == 0:
                        split_stands(groups["mem"] + s)
                    slot(4 * b + s, 0, b, mT_hi, mT_lo, 4 * s, 4, NW, s == 0, s == 3)
                    if b == 0 and s < 2:
                        turn_mem(2 + s)
                    if b == 0 and s == 2:
                        pe.wait_ge(rows_in, 16 * (len(GAIN_ROWS) - 1))
                        R = N_ROWS - KD
                        nc.tensor.transpose(small[:, 1, 0:R], rows[0:R, :], ident[0:R, 0:R]).then_inc(ev("gains_turned"), 1)
                    if 3 <= 4 * b + s < 3 + DB:
                        j = 4 * b + s - 3
                        if j == 0:
                            pe.wait_ge(x_in, 16 * TT)
                        turn_features(groups["x"] + j, 0, of(x, j * NW))
            split_stands(groups["x"] + DB - 1)
            ffn(1, "x1")

            def step(k):
                h, l = divmod(k, STEPS)
                if l == 0:
                    pe.wait_ge(ev("complement"), h + 1)
                    split_stands(groups[f"hq{h}"])
                else:
                    pe.wait_ge(ev("waves"), h * (STEPS - 1) + l)
                w = wave[:, k % 2, :].rearrange("p (h t) -> p h t", h=HH)
                for b in range(2):
                    fill(fills["steps"] + k, b)
                    N = HALF if 0 < l < LEVELS else P
                    for n in range(HH if l < LEVELS else HH // 2):
                        if l == 0:
                            keys, queries = kxT[:, n, b * P:(b + 1) * P], qxT[:, n, b * P:(b + 1) * P]
                        elif l < LEVELS:
                            keys = w[:, n, b * P:(b + 1) * P]
                            queries = uppers(keys, l)
                        else:
                            keys, queries = w[:, 2 * b + n, 0:P], w[:, 2 * b + n, P:2 * P]
                        ins = mm(small[:, b, n * N:(n + 1) * N], keys, queries, start=True, stop=True)
                    ins.then_inc(small_ready[b], 1)

            def mixer(m):
                if m < 4:
                    entry("x2", m)
                if m % 4 == 0 and m:
                    b = m // 4 - 1
                    n = MIX[b] if b < len(MIX) else ""
                    if n in groups:
                        stands(blocks["mix"] + b)
                        src, tiles = {"hf": (gate, 4), "hq": (nat, 4), "cq": (gate, QR), "ck": (ckv_nat, KR)}[n[:2]]
                        turn_features(groups[n], 0, of(src), tiles)
                for h in range(2):
                    if 0 <= m - STEP0[h] < STEPS:
                        step(h * STEPS + m - STEP0[h])
                    if m == 40 + 2 * h:
                        recurrence_outputs(h)

            def recurrence_outputs(h):
                f = fills["av"] + h
                B = blocks["mix"] + MIX.index("hi1")
                stands(B)
                for t in range(TT):
                    fill(f, t)
                    for n in range(HH):
                        head = h * HH + n
                        dst = small[:, t, n * P:(n + 1) * P]
                        v = slice(head * P, (head + 1) * P)
                        ins = mm(dst, AT[:, head, t, :], V[:, t, v], start=True, stop=t == 0)
                        if t == 1:
                            ins = mm(dst, AT[:, head, 2, :], V[:, 0, v], start=False, stop=True)
                    ins.then_inc(small_ready[t], 1)

            for m in range(40):
                B = blocks["mix"] + m // 4
                if m % 4 == 0:
                    free(B)
                slot(M + m, 0, B, hT_hi, hT_lo, 4 * (m % 4), 4, MIX_WIDTH[MIX[m // 4]], m % 4 == 0, m % 4 == 3)
                mixer(m)
            for b in range(3):
                if b == 0:
                    split_stands(groups["cq"])
                free(blocks["q_up"] + b)
                slot(slots["q_up"] + b, 0, blocks["q_up"] + b, cqT_hi, cqT_lo, 0, QR, NW, True, True)
                mixer(40 + b)
            for b in range(2):
                if b == 0:
                    split_stands(groups["ckv"])
                for n in range(2):
                    B = blocks["kv_up"] + 2 * b + n
                    free(B)
                    slot(slots["kv_up"] + b, 0, B, ckvT_hi, ckvT_lo, 0, KR, NW, True, True, off=n * NW, full=2 * NW, signal=n == 1)
                mixer(43 + b)

            def recurrence_slot(k):
                B = blocks["w_out_hg"] + k // 2
                if k % 2 == 0:
                    free(B)
                slot(slots["w_out_hg"] + k, 0, B, catT_hi, catT_lo, 8 + 4 * (k % 2), 4, NW, k % 2 == 0, k % 2 == 1)

            pe.wait_ge(ev("hg_scaled"), 1)
            for i in range(2):
                turn_features(groups["cat_hg"] + i, 0, of(o_hg, i * NW))
            split_stands(groups["cat_hg"])
            recurrence_slot(0)
            pe.wait_ge(ev("q_scaled"), 1)
            for i in range(2):
                turn_features(groups["qn"] + i, 0, lambda m, t: q_nat[:, t, (4 * i + m) * QK:(4 * i + m) * QK + P])
            recurrence_slot(1)
            pe.wait_ge(ev("k_scaled"), 1)
            for i in range(2):
                turn_features(groups["kn"] + i, 0, lambda m, t: kv_nat[:, t, (4 * i + m) * 2 * P:(4 * i + m) * 2 * P + P])
            recurrence_slot(2)
            pe.wait_ge(ev("q_rotated"), 1)
            turn_features(groups["qp"], 0, lambda m, t: q_pe[:, t, 2 * m:2 * m + 2, :].rearrange("p h c -> p (h c)"))
            pe.wait_ge(ev("k_rotated"), 1)
            turn_features(groups["kp"], 0, lambda m, t: k_pe[:, t, 2 * m:2 * m + 2, :].rearrange("p h c -> p (h c)"))
            recurrence_slot(3)

            score_fill, out_fill = FILL_ORDER

            def scores(p):
                f = fills["mla"] + score_fill[p]
                for b, (t, keys) in enumerate(((1, SEQ), (0, P))):
                    fill(f, b)
                    for n in range(2):
                        h = 2 * p + n
                        dst = small[:, b, n * keys:(n + 1) * keys]
                        mm(dst, qTn[:, h, t * P:(t + 1) * P], kTn[:, h, 0:keys], start=True, stop=False)
                        ins = mm(dst, qTp[n][:, p, t * P:(t + 1) * P], kTp[:, p, 0:keys], start=False, stop=True)
                    ins.then_inc(small_ready[b], 1)

            def probs(p):
                s = flat_stage[:, (p % 2) * 1024:(p % 2) * 1024 + 6 * P]
                pe.wait_ge(ev("exps"), p + 1)
                turn(groups["prob"] + p, 0, [[s[:, n * P:(n + 1) * P] for n in ns] for ns in (range(4), range(4, 6))])

            def outputs(p):
                f = fills["mla"] + out_fill[p]
                split_stands(groups["prob"] + p)
                pT = probT[:, p % 2, :]
                for b in range(2):
                    fill(f, b)
                    for n in range(2):
                        h = 2 * p + n
                        dst = small[:, b, n * P:(n + 1) * P]
                        for k in range(2 - b):
                            c = (2 * n + k) * P if b == 0 else (4 + n) * P
                            ins = mm(dst, pT[:, c:c + P], kv_nat[:, k, h * 2 * P + P:(h + 1) * 2 * P], start=k == 0, stop=k == 1 - b)
                    ins.then_inc(small_ready[b], 1)

            flat_stage = stage[:].rearrange("p a b -> p (a b)")
            split_stands(groups["kp"])
            scores(0)
            recurrence_slot(4)
            scores(1)
            probs(0)
            scores(2)
            outputs(0)
            probs(1)
            recurrence_slot(5)
            scores(3)
            outputs(1)
            probs(2)
            outputs(2)
            recurrence_slot(6)
            probs(3)
            outputs(3)
            recurrence_slot(7)

            pe.wait_ge(ev("o_scaled"), 1)
            for i in range(2):
                turn_features(groups["cat_mla"] + i, 0, of(o_mla, i * NW))
            split_stands(groups["cat_mla"])
            for j in range(DB):
                B = blocks["w_out"] + j
                free(B)
                for s in range(2):
                    if j == 0 and s == 1:
                        split_stands(groups["cat_mla"] + 1)
                    slot(slots["w_out"] + 2 * j + s, 0, B, catT_hi, catT_lo, 4 * s, 4, NW, s == 0, s == 1)
                    if j and s == 0:
                        stands(B - 1)
                        turn_features(groups["x_out"] + j - 1, 0, of(x, (j - 1) * NW))

            B = blocks["xq"]
            free(B)
            for s in range(4):
                slot(slots["xq"] + s, 0, B, hT_hi, hT_lo, 4 * s, 4, NW, s == 0, s == 3)
                entry("x3", s)
            pe.wait_ge(ev("xq_scaled"), 1)
            turn_features(groups["xq"], 0, of(gate))
            split_stands(groups["xq"])
            for p in range(XH // 2):
                for t in range(TT):
                    fill(fills["xattn"] + p, t)
                    for n in range(2):
                        ins = mm(small[:, t, n * MEM:(n + 1) * MEM], xqT[:, 2 * p + n, t * P:(t + 1) * P], memkT[:, 2 * p + n, :], start=True, stop=True)
                    ins.then_inc(small_ready[t], 1)
            for p in range(XH // 2):
                pe.wait_ge(ev("x_exps"), p + 1)
                turn(groups["x_prob"] + p, 0, [[stage[:, 2 * p + t, n * P:(n + 1) * P] for n in range(4)] for t in range(TT)])
            for p in range(XH // 2):
                split_stands(groups["x_prob"] + p)
                for t in range(TT):
                    fill(fills["xattn"] + XH // 2 + p, t)
                    for n in range(2):
                        for k in range(MT):
                            c = (2 * n + k) * P
                            ins = mm(small[:, t, n * P:(n + 1) * P], x_probT[:, p, t, c:c + P],
                                     memv[:, k, (2 * p + n) * P:(2 * p + n + 1) * P], start=k == 0, stop=k == MT - 1)
                    ins.then_inc(small_ready[t], 1)
            for t in range(TT):
                pe.wait_ge(small_taken[t], fills["xattn"] + XH)
            turn_features(groups["xo"], 0, of(xo))
            split_stands(groups["xo"])
            for j in range(DB):
                B = blocks["w_o"] + j
                free(B)
                slot(slots["w_o"] + j, 0, B, xoT_hi, xoT_lo, 0, 4, NW, True, True)
                if j >= 2:
                    stands(B - 2)
                    turn_features(groups["x_o"] + j - 2, 0, of(x, (j - 2) * NW))
            stands(blocks["w_o"] + DB - 2)
            turn_features(groups["x_o"] + DB - 2, 0, of(x, (DB - 2) * NW))
            ffn(2, "x4")


_INS = ["x", "mem", "positions", "ffn1_norm", "ffn1_w_gate", "ffn1_w_up", "ffn1_w_down", "mix_norm", "w_in", "mla_q_a_norm", "mla_w_q_up",
        "mla_kv_a_norm", "mla_w_kv_up", "mla_q_norm", "mla_k_norm", "mla_out_norm", "hg_lb_logits", "hg_out_norm", "w_out", "xattn_norm",
        "mem_norm", "xattn_w_q", "xattn_w_kv", "xattn_q_norm", "xattn_k_norm", "xattn_w_o", "ffn2_norm", "ffn2_w_gate", "ffn2_w_up",
        "ffn2_w_down"]


def constants():
    s, t = np.arange(P)[:, None], np.arange(P)[None, :]
    level_mask = np.zeros((P, LEVELS, P), np.int32)
    for level in range(1, LEVELS):
        m = 2 ** (level - 1)
        level_mask[:, level, :] = (s // (2 * m) == t // (2 * m)) & (s // m % 2 == 0) & (t // m % 2 == 1)
    causal = np.zeros((P, 2 * P), np.float32)
    causal[:, P:] = np.where(t <= s, 0.0, -1e30)
    freq = np.float32(10000.0) ** (-np.arange(RH, dtype=np.float32) / np.float32(RH))
    return {"ident": np.eye(P, dtype=np.float32), "level_mask": level_mask, "causal": causal,
            "freq": np.ascontiguousarray(np.broadcast_to(freq.astype(np.float32), (P, RH)))}


def kernel(**inputs):
    import concourse.bacc as bacc
    from concourse.bass_utils import run_bass_kernel_spmd

    nc = bacc.Bacc("TRN2", target_bir_lowering=False, num_devices=1)
    data = {n: np.ascontiguousarray(inputs[n]) for n in _INS}
    data.update(constants())
    arrays, args = {}, {}
    for n, v in data.items():
        arrays[f"in_{n}"] = v
        args[n] = nc.dram_tensor(f"in_{n}", v.shape, mybir.dt.from_np(v.dtype), kind="ExternalInput").ap()
    out = nc.dram_tensor("out_0", data["x"].shape, F32, kind="ExternalOutput").ap()
    layer(nc, args, out)
    r = run_bass_kernel_spmd(nc, [arrays], core_ids=[0])
    return r.results[0]["out_0"]
```
